# Optimizing a Trainium2 kernel written in Bass

```python
import math
import jax, jax.numpy as jnp
from jax import lax
import numpy as np

D_MODEL = 1024
BATCH = 1
SEQ = 256
DEPTH = 2

N_MIXERS = 2
N_SSM_LAYERS = (DEPTH + 1) // 2
N_ATTN_LAYERS = DEPTH // 2
RMS_EPS = 1e-6

SSM_GROUP = 16
SSM_GROUPS = D_MODEL // SSM_GROUP
SSM_STATE = 64
STEP_MIN = 1e-3
STEP_MAX = 1e-1

ATTN_HEAD_DIM = 64
ATTN_HEADS = D_MODEL // ATTN_HEAD_DIM
DILATED_GROUPS = ((128, 1), (512, 4), (2048, 16))
N_DIL_GROUPS = len(DILATED_GROUPS)
QKV_COLS = N_DIL_GROUPS * 3 * ATTN_HEADS * ATTN_HEAD_DIM
ATTN_BLOCK = 128
ROPE_THETA = 10000.0

PEER_HEADS = 8
PEER_N_KEYS = 128
PEER_N_EXPERTS = PEER_N_KEYS * PEER_N_KEYS
PEER_KEY_DIM = 256
PEER_HALF = PEER_KEY_DIM // 2
PEER_TOPK = 16
PEER_CHUNK = 128

kernel_name = "hybrid_s5_dilated_attn_peer"

def rms_norm(x, g):
    xf = x.astype(jnp.float32)
    y = xf * lax.rsqrt(jnp.mean(xf * xf, axis=-1, keepdims=True) + RMS_EPS)
    return (y * g.astype(jnp.float32)).astype(x.dtype)

def _complex_affine_combine(left, right):
    a1r, a1i, b1r, b1i = left
    a2r, a2i, b2r, b2i = right
    ar = a2r * a1r - a2i * a1i
    ai = a2r * a1i + a2i * a1r
    br = a2r * b1r - a2i * b1i + b2r
    bi = a2r * b1i + a2i * b1r + b2i
    return (ar, ai, br, bi)

def s5_mixer(h, lam_re, lam_im, log_step, b_re, b_im, c_re, c_im, d_skip, w_glu):
    f32 = jnp.float32
    bsz, seq, _ = h.shape
    u = h.astype(f32).reshape(bsz, seq, SSM_GROUPS, SSM_GROUP)
    lam_re = lam_re.astype(f32)
    lam_im = lam_im.astype(f32)
    step = jnp.exp(log_step.astype(f32))[:, None]
    mag = jnp.exp(lam_re * step)
    lb_re = mag * jnp.cos(lam_im * step)
    lb_im = mag * jnp.sin(lam_im * step)
    den = lam_re * lam_re + lam_im * lam_im
    num_re = lb_re - 1.0
    coef_re = (num_re * lam_re + lb_im * lam_im) / den
    coef_im = (lb_im * lam_re - num_re * lam_im) / den
    b_re = b_re.astype(f32)
    b_im = b_im.astype(f32)
    bb_re = coef_re[..., None] * b_re - coef_im[..., None] * b_im
    bb_im = coef_re[..., None] * b_im + coef_im[..., None] * b_re
    bu_re = jnp.einsum('blgh,gph->lbgp', u, bb_re)
    bu_im = jnp.einsum('blgh,gph->lbgp', u, bb_im)
    a_re = jnp.broadcast_to(lb_re, (seq, 1, SSM_GROUPS, SSM_STATE))
    a_im = jnp.broadcast_to(lb_im, (seq, 1, SSM_GROUPS, SSM_STATE))
    _, _, s_re, s_im = lax.associative_scan(_complex_affine_combine,
                                            (a_re, a_im, bu_re, bu_im), axis=0)
    y = (jnp.einsum('lbgp,ghp->blgh', s_re, c_re.astype(f32))
         - jnp.einsum('lbgp,ghp->blgh', s_im, c_im.astype(f32)))
    y = y.reshape(bsz, seq, D_MODEL) + d_skip.astype(f32) * h.astype(f32)
    y = jax.nn.gelu(y).astype(h.dtype)
    z = y @ w_glu
    val, gate = jnp.split(z, 2, axis=-1)
    return val * jax.nn.sigmoid(gate)

def rope(x, positions):
    dh = x.shape[-1]
    half = dh // 2
    inv = ROPE_THETA ** (-jnp.arange(half, dtype=jnp.float32) / half)
    ang = positions.astype(jnp.float32)[:, None] * inv[None, :]
    cos = jnp.cos(ang)[None, :, None, :]
    sin = jnp.sin(ang)[None, :, None, :]
    xf = x.astype(jnp.float32)
    x1, x2 = xf[..., :half], xf[..., half:]
    return jnp.concatenate([x1 * cos - x2 * sin, x2 * cos + x1 * sin], axis=-1).astype(x.dtype)

def dilated_window_attention(q, k, v, dilation, window):
    bsz, seq, nh, dh = q.shape
    m_len = seq // dilation
    c = min(ATTN_BLOCK, m_len)
    nblk = m_len // c
    steps = window // dilation

    def to_residues(t):
        return t.reshape(bsz, m_len, dilation, nh, dh).transpose(0, 2, 1, 3, 4)

    def band(t):
        tp = jnp.pad(t, ((0, 0), (0, 0), (c, 0), (0, 0), (0, 0)))
        tb = tp.reshape(bsz, dilation, nblk + 1, c, nh, dh)
        return jnp.concatenate([tb[:, :, :-1], tb[:, :, 1:]], axis=3)

    qb = to_residues(q).reshape(bsz, dilation, nblk, c, nh, dh)
    kb = band(to_residues(k))
    vb = band(to_residues(v))
    s = jnp.einsum('bdnqhe,bdnkhe->bdnhqk', qb, kb).astype(jnp.float32) * (dh ** -0.5)
    qi = jnp.arange(c)[:, None]
    ki = jnp.arange(2 * c)[None, :]
    dist = qi + c - ki
    blk = jnp.arange(nblk)[:, None, None]
    valid = (dist >= 0) & (dist <= steps) & (blk * c + ki - c >= 0)
    s = jnp.where(valid[:, None], s, -1e30)
    smax = jnp.max(s, axis=-1, keepdims=True)
    e = jnp.exp(s - smax)
    den = jnp.sum(e, axis=-1, keepdims=True)
    p = (e / den).astype(v.dtype)
    lse = smax[..., 0] + jnp.log(den[..., 0])
    o = jnp.einsum('bdnhqk,bdnkhe->bdnqhe', p, vb)
    o = o.transpose(0, 2, 3, 1, 4, 5).reshape(bsz, seq, nh, dh)
    lse = lse.transpose(0, 2, 4, 1, 3).reshape(bsz, seq, nh)
    return o, lse

def dilated_attention_mixer(h, w_qkv, w_o):
    bsz, seq, _ = h.shape
    qkv = (h @ w_qkv).reshape(bsz, seq, N_DIL_GROUPS, 3, ATTN_HEADS, ATTN_HEAD_DIM)
    pos = jnp.arange(seq)
    outs, lses = [], []
    for g, (window, dilation) in enumerate(DILATED_GROUPS):
        q = rope(qkv[:, :, g, 0], pos)
        k = rope(qkv[:, :, g, 1], pos)
        v = qkv[:, :, g, 2]
        o, lse = dilated_window_attention(q, k, v, dilation, window)
        outs.append(o)
        lses.append(lse)
    wts = jax.nn.softmax(jnp.stack(lses, axis=0), axis=0).astype(h.dtype)
    o = jnp.einsum('gblh,gblhe->blhe', wts, jnp.stack(outs, axis=0))
    return o.reshape(bsz, seq, ATTN_HEADS * ATTN_HEAD_DIM) @ w_o

def peer_ffn(h, w_q, sub_keys, u_tab, v_tab):
    bsz, seq, d = h.shape
    q = (h @ w_q).reshape(bsz, seq, PEER_HEADS, 2, PEER_HALF)
    s = jnp.einsum('blhpe,hpne->blhpn', q, sub_keys).astype(jnp.float32)
    s_top, i_top = lax.top_k(s, PEER_TOPK)
    cand = (s_top[..., 0, :, None] + s_top[..., 1, None, :]).reshape(bsz, seq, PEER_HEADS, -1)
    cand_idx = (i_top[..., 0, :, None] * PEER_N_KEYS + i_top[..., 1, None, :]).reshape(
        bsz, seq, PEER_HEADS, -1)
    best, pos = lax.top_k(cand, PEER_TOPK)
    idx = jnp.take_along_axis(cand_idx, pos, axis=-1)
    gate = jax.nn.softmax(best, axis=-1).astype(h.dtype)
    ntok = bsz * seq
    nchunk = ntok // PEER_CHUNK
    kk = PEER_HEADS * PEER_TOPK
    h_c = h.reshape(nchunk, PEER_CHUNK, d)
    i_c = idx.reshape(nchunk, PEER_CHUNK, kk)
    g_c = gate.reshape(nchunk, PEER_CHUNK, kk)

    def chunk_fn(args):
        hc, ic, gc = args
        act = jnp.einsum('cd,ckd->ck', hc, u_tab[ic])
        return jnp.einsum('ck,ckd->cd', gc * jax.nn.gelu(act), v_tab[ic])

    out = lax.map(chunk_fn, (h_c, i_c, g_c))
    return out.reshape(bsz, seq, d)

def setup_inputs(seed: int = 0) -> dict:
    key = jax.random.key(seed)
    ks = jax.random.split(key, 20)
    f32 = jnp.float32
    nrm = jax.random.normal
    nA, nB = N_SSM_LAYERS, N_ATTN_LAYERS
    G, P, H = SSM_GROUPS, SSM_STATE, SSM_GROUP
    x = nrm(ks[0], (BATCH, SEQ, D_MODEL), f32)
    norm_mix = 1.0 + 0.02 * nrm(ks[1], (DEPTH, D_MODEL), f32)
    norm_ffn = 1.0 + 0.02 * nrm(ks[2], (DEPTH, D_MODEL), f32)
    norm_final = 1.0 + 0.02 * nrm(ks[3], (D_MODEL,), f32)
    s5_lam_re = -0.5 + 0.01 * nrm(ks[4], (nA, G, P), f32)
    s5_lam_im = jnp.pi * jnp.arange(P, dtype=f32) + 0.01 * nrm(ks[5], (nA, G, P), f32)
    s5_log_step = jax.random.uniform(ks[6], (nA, G), f32,
                                     minval=math.log(STEP_MIN), maxval=math.log(STEP_MAX))
    s5_b_re = nrm(ks[7], (nA, G, P, H), f32) * (2 * H) ** -0.5
    s5_b_im = nrm(ks[8], (nA, G, P, H), f32) * (2 * H) ** -0.5
    s5_c_re = nrm(ks[9], (nA, G, H, P), f32) * (2 * P) ** -0.5
    s5_c_im = nrm(ks[10], (nA, G, H, P), f32) * (2 * P) ** -0.5
    s5_d = nrm(ks[11], (nA, D_MODEL), f32)
    s5_w_glu = nrm(ks[12], (nA, D_MODEL, 2 * D_MODEL), f32) * D_MODEL ** -0.5
    attn_w_qkv = nrm(ks[13], (nB, D_MODEL, QKV_COLS), f32) * D_MODEL ** -0.5
    attn_w_o = nrm(ks[14], (nB, ATTN_HEADS * ATTN_HEAD_DIM, D_MODEL), f32) * (
        ATTN_HEADS * ATTN_HEAD_DIM) ** -0.5
    peer_w_q = nrm(ks[15], (DEPTH, D_MODEL, PEER_HEADS * PEER_KEY_DIM), f32) * D_MODEL ** -0.5
    peer_sub_keys = nrm(ks[16], (DEPTH, PEER_HEADS, 2, PEER_N_KEYS, PEER_HALF), f32) * PEER_HALF ** -0.5
    peer_u = nrm(ks[17], (DEPTH, PEER_N_EXPERTS, D_MODEL), f32) * D_MODEL ** -0.5
    peer_v = nrm(ks[18], (DEPTH, PEER_N_EXPERTS, D_MODEL), f32) * PEER_HEADS ** -0.5
    return {"x": x, "norm_mix": norm_mix, "norm_ffn": norm_ffn, "norm_final": norm_final,
            "s5_lam_re": s5_lam_re, "s5_lam_im": s5_lam_im, "s5_log_step": s5_log_step,
            "s5_b_re": s5_b_re, "s5_b_im": s5_b_im, "s5_c_re": s5_c_re, "s5_c_im": s5_c_im,
            "s5_d": s5_d, "s5_w_glu": s5_w_glu, "attn_w_qkv": attn_w_qkv, "attn_w_o": attn_w_o,
            "peer_w_q": peer_w_q, "peer_sub_keys": peer_sub_keys, "peer_u": peer_u,
            "peer_v": peer_v}

def reference(x, norm_mix, norm_ffn, norm_final, s5_lam_re, s5_lam_im, s5_log_step,
              s5_b_re, s5_b_im, s5_c_re, s5_c_im, s5_d, s5_w_glu, attn_w_qkv, attn_w_o,
              peer_w_q, peer_sub_keys, peer_u, peer_v):
    for i in range(DEPTH):
        h = rms_norm(x, norm_mix[i])
        j = i // N_MIXERS
        if i % N_MIXERS == 0:
            mix = s5_mixer(h, s5_lam_re[j], s5_lam_im[j], s5_log_step[j], s5_b_re[j],
                           s5_b_im[j], s5_c_re[j], s5_c_im[j], s5_d[j], s5_w_glu[j])
        else:
            mix = dilated_attention_mixer(h, attn_w_qkv[j], attn_w_o[j])
        x = x + mix
        h = rms_norm(x, norm_ffn[i])
        x = x + peer_ffn(h, peer_w_q[i], peer_sub_keys[i], peer_u[i], peer_v[i])
    return rms_norm(x, norm_final)


_drawn_inputs = setup_inputs


def setup_inputs(seed=0):
    import zlib

    import numpy as np

    out = dict(_drawn_inputs(seed))
    spreads = {}
    factors = {}
    for name, (base, spread) in spreads.items():
        noise = np.random.default_rng([zlib.crc32(name.encode()), seed]).standard_normal(out[name].shape)
        drawn = base * np.exp(spread * noise) if base else spread * noise
        out[name] = __import__('jax').numpy.asarray(drawn.astype(out[name].dtype))
    for name, factor in factors.items():
        out[name] = (out[name] * factor).astype(out[name].dtype)
    return out
```

```python
from contextlib import ExitStack

import numpy as np

import concourse.bass as bass
from concourse import mybir

F32 = mybir.dt.float32
U32 = mybir.dt.uint32
ALU = mybir.AluOpType
ACT = mybir.ActivationFunctionType
AX = mybir.AxisListType

P = 128
D = 1024
SEQ = 256
NC = SEQ // P
KT = D // P
EPS = 1e-6
GROUPS, STATE, GH = 64, 64, 16
PAIRS = GROUPS // 2
PPT = PAIRS // KT
HEADS, DH = 16, 64
DILATED = ((128, 1), (512, 4), (2048, 16))
NG = len(DILATED)
PH, NKEYS, TOPK = 8, 128, 16
HP = 2 * PH
STEPS = PH * TOPK
RING = 8
SETS = RING // 2
PAIRS_G = STEPS // 2
ROUNDS = STEPS // RING
BLOCK = 512
NH = HEADS // 2
NEG = -3.0e38
MASKED = -8.0e30
TWO_PI = 6.283185
HALF_PI = 1.5707963
ROUND = 12582912.0

GLU, WQ0, ITEMS0 = 0, 4, 8
QKV, WO, WQ1, ITEMS1 = 0, 18, 20, 24

C_ID, C_RAMP, C_IOTA, C_COS, C_SIN, C_ALL = 0, 128, 256, 272, 400, 528
M_AT = (0, NG * P)
M_ALL = NG * P + NG * 2 * P
A_WORDS = 18176
A_TOPK = 6144


def item(layer, c, i):
    return (ITEMS0 * c if layer == 0 else NC * ITEMS0 + ITEMS1 * c) + i


def norm_event(layer, c, ffn):
    return 4 * layer + 2 * c + ffn


def build(nc, x, gains, lam, b_in, c_out, d_skip, w_glu, w_qkv, w_o, w_q, keys, experts, consts,
          masks, out):
    ctx = ExitStack()
    with ctx:
        def sb(name, shape, dt=F32):
            return ctx.enter_context(nc.sbuf_tensor(name, shape, dt))

        def sem(name):
            return ctx.enter_context(nc.semaphore(name))

        X = sb("X", [P, NC, D])
        H = sb("H", [P, NC, D])
        hT = sb("hT", [P, KT, P])
        gT = sb("gT", [P, KT, P])
        gain = sb("gain", [P, D])
        wt = sb("wt", [P, 2, KT, BLOCK])
        ringmem = sb("ringmem", [P, RING * 2 * D])
        area = sb("area", [P, A_WORDS])
        con = sb("con", [P, C_ALL])
        row_a = sb("row_a", [P, NC, STEPS], U32)
        row_b = sb("row_b", [P, NC, STEPS], U32)
        gate = sb("gate", [P, NC, STEPS])
        rows_now = sb("rows_now", [P, SETS, 2], U32)
        tick = sb("tick", [P, 1], U32)
        dots = sb("dots", [P, RING])
        gelus = sb("gelus", [P, RING])
        wts = sb("wts", [P, RING])
        diag = sb("diag", [P, SETS, P])
        stat = sb("stat", [P, 8])
        half_pi = sb("half_pi", [P, 1])
        mx = sb("mx", [P, NC * HEADS])
        nmx = sb("nmx", [P, NC * HEADS])
        den = sb("den", [P, NC * HEADS])
        rden = sb("rden", [P, NC * HEADS])
        skip = sb("skip", [P, KT])
        ps = ctx.enter_context(nc.psum_tensor("ps", [P, 8, 512], F32))

        ident = con[:, C_ID:C_ID + P]
        ramp = con[:, C_RAMP:C_RAMP + P]
        iota = con[:, C_IOTA:C_IOTA + TOPK]

        def banks(a, b):
            return ps[:, a:b, :].rearrange("p b n -> p (b n)")

        def view(t, at, *shape):
            n = int(np.prod(shape))
            v = t[:, at:at + n]
            if len(shape) == 2:
                v = v.rearrange("p (a b) -> p a b", a=shape[0])
            if len(shape) == 3:
                v = v.rearrange("p (a b c) -> p a b c", a=shape[0], b=shape[1])
            return v

        def spread(ap, axis, shape):
            return ap.unsqueeze(axis).to_broadcast(shape)

        cosT = view(area, 0, PAIRS, P)
        sinT = view(area, 4096, PAIRS, P)
        WB = view(area, 8192, KT, 2, P)
        CW = view(area, 10240, PAIRS, 3, 32)
        M = [[view(area, 13312 + (4 * p + i) * 512, PPT, P) for i in range(4)] for p in range(2)]
        mag, z0re, z0im, zta, ztb = [view(area, 17408 + 32 * i, PAIRS) for i in range(5)]
        sig = view(area, 13312, D)
        craw = view(ringmem, 0, 2, PAIRS, GH)
        tmpc = view(ringmem, 1024, 2, PAIRS, GH)
        small = view(ringmem, 2048, 20, PAIRS)
        (lre, lim, step, xr, turn, whole, frac, sn, cs, lbre, lbim, dn, rdn, ta, tb, cre, cim,
         absf) = [small[:, i, :] for i in (0, 1, 3, 4, 5, 6, 7, 8, 9, 10, 11, 12, 13, 14, 15, 16, 17, 18)]

        class TopK:
            def __init__(self, t, at):
                self.keysT = view(t, at, HP, NKEYS)
                self.qT = view(t, at + 2048, HP, P)
                self.S = view(t, at + 4096, HP, NKEYS)
                self.S2 = view(t, at + 6144, HP, NKEYS)
                self.EQ = view(t, at + 8192, STEPS, TOPK)
                at += 10240
                self.stop = view(t, at, HP, TOPK)
                self.itop = view(t, at + 256, HP, TOPK).bitcast(U32)
                self.itopf = view(t, at + 512, HP, TOPK)
                (self.best, pos, posi, posj, self.posif, self.posjf) = [
                    view(t, at + 768 + 128 * i, PH, TOPK) for i in range(6)]
                self.pos, self.posi, self.posj = [a.bitcast(U32) for a in (pos, posi, posj)]
                self.keyf = view(t, at + 1536, STEPS)
                self.gsum = view(t, at + 1664, PH)
                self.grec = view(t, at + 1672, PH)

        topk_in = [TopK(ringmem, 4096)] + [TopK(area, A_TOPK)] * 3

        K0 = view(area, 0, NG, 8, P)
        V0 = view(area, 3072, NG, D)
        K1 = view(area, 6144, NG, 4, P)
        V1 = view(area, 7680, NG, BLOCK)
        QT = view(area, 9216, NG, 4, P)
        RA = view(area, 10752, BLOCK)
        RB = view(area, 11264, BLOCK)
        RR = [view(area, 11776 + BLOCK * i, BLOCK) for i in range(2)]
        mask = view(area, 12800, 2 * NG * P)
        SS = [view(area, 13568 + 768 * i, 768) for i in range(2)]
        PT = [view(area, 15104 + 768 * i, 768) for i in range(2)]
        O = view(area, 16640, D)
        ring = view(ringmem, 0, RING, 2 * D)

        x_in = [sem(f"x_in{c}") for c in range(NC)]
        con_in = sem("con_in")
        lam_in = sem("lam_in")
        craw_in = sem("craw_in")
        zeroed = sem("zeroed")
        wb_in = sem("wb_in")
        gain_in = sem("gain_in")
        keys_in = sem("keys_in")
        mask_in = sem("mask_in")
        w_in = [sem(f"w_in{k}") for k in range(2)]
        w_used = sem("w_used")
        dve = sem("dve_step")
        act_step = sem("act_step")
        var_ready = sem("var_ready")
        root_ready = sem("root_ready")
        normed = sem("normed")
        turned = sem("turned")
        hT_ready = sem("hT_ready")
        lam_dve = sem("lam_dve")
        lam_act = sem("lam_act")
        tab_dve = sem("tab_dve")
        tab_act = sem("tab_act")
        cw_ready = sem("cw_ready")
        bu_ready = sem("bu_ready")
        bu_used = sem("bu_used")
        prod_ready = sem("prod_ready")
        y_ready = sem("y_ready")
        y_skip = sem("y_skip")
        y_gelu = sem("y_gelu")
        sig_ready = sem("sig_ready")
        glu_done = sem("glu_done")
        q_copied = sem("q_copied")
        score_done = sem("score_done")
        score_copied = sem("score_copied")
        best_ready = sem("best_ready")
        gate_exp = sem("gate_exp")
        idx_ready = sem("idx_ready")
        rows_ready = sem("rows_ready")
        landed = [sem(f"landed{i}") for i in range(RING)]
        dots_ready = sem("dots_ready")
        gelu_ready = sem("gelu_ready")
        wts_ready = sem("wts_ready")
        diag_ready = sem("diag_ready")
        v_pe = sem("v_pe")
        v_dve = sem("v_dve")
        peer_done = sem("peer_done")
        acc_evac = sem("acc_evac")
        roped = sem("roped")
        qk_turned = sem("qk_turned")
        qk_copied = sem("qk_copied")
        s_done = sem("s_done")
        s_masked = sem("s_masked")
        nmx_ready = sem("nmx_ready")
        p_ready = sem("p_ready")
        p_turned = sem("p_turned")
        pT_copied = sem("pT_copied")
        pv_done = sem("pv_done")
        o_scaled = sem("o_scaled")
        o_turned = sem("o_turned")
        oT_ready = sem("oT_ready")
        wo_done = sem("wo_done")
        out_ready = sem("out_ready")
        out_done = sem("out_done")

        block = ctx.enter_context(nc.Block())

        class Gather:

            def __init__(self, eng, pair):
                self.eng, self.pair, self.done = eng, pair, 0

            def at(self, phase, n):
                if phase is None:
                    return
                upto = PAIRS_G * phase + min(n, PAIRS_G)
                while self.done < upto:
                    b, r = divmod(self.done, SETS)
                    last = (upto // SETS if upto % PAIRS_G else upto // SETS - 1)
                    if r == 0 and b % ROUNDS and last - b >= 2:
                        with self.eng.Fori(b, last) as i:
                            for r in range(SETS):
                                self.pair(r, i, phase, i - phase * ROUNDS, False, False)
                        self.done = last * SETS
                        continue
                    self.pair(r, b, phase, b - phase * ROUNDS, self.done % PAIRS_G == 0,
                              self.done % PAIRS_G == PAIRS_G - 1)
                    self.done += 1

        S5_K, S5_END = 3, 26
        GLU_AT, NORM1_AT, WQ_AT, SCORE_AT, TOPK_AT = 26, 31, 35, 39, 41
        A_QKV, A_HEADS, A_HALF = 6, 17, 23
        A_WO, A_NORM, A_WQ, A_SCORE, A_TOPK_AT = 52, 55, 58, 62, 64

        @block.sync
        def _(sp):
            sp.dma_start(X[:, 0, :], x[0:P, :]).then_inc(x_in[0], 16)
            sp.dma_start(small[:, 0:3, :], lam).then_inc(lam_in, 16)
            sp.dma_start(con[:, :], consts).then_inc(con_in, 16)
            sp.dma_start(skip[:, :], d_skip).then_inc(lam_in, 16)
            sp.dma_start(gain[:, :], gains[0:1, :].to_broadcast([P, D])).then_inc(gain_in, 16)
            sp.dma_start(craw[:, :, :, :], c_out).then_inc(craw_in, 16)
            sp.wait_ge(zeroed, 1)
            for g in range(KT):
                for r in range(2):
                    a = g % 2
                    sp.dma_start(WB[GH * g:GH * (g + 1), :, r, a * STATE:(a + 1) * STATE],
                                 b_in[r, g]).then_inc(wb_in, 16)
            sp.dma_start(X[:, 1, :], x[P:2 * P, :]).then_inc(x_in[1], 16)

            def weights(layer, c, first, last):
                for i in range(first, last):
                    n = item(layer, c, i)
                    if layer == 0:
                        src = (w_glu[:, i * BLOCK:(i + 1) * BLOCK] if i < WQ0 else
                               w_q[0, :, (i - WQ0) * BLOCK:(i - WQ0 + 1) * BLOCK])
                    elif i < WO:
                        half, j = divmod(i, 9)
                        src = w_qkv[:, j * D + half * BLOCK:j * D + (half + 1) * BLOCK]
                    elif i < WQ1:
                        src = w_o[:, (i - WO) * BLOCK:(i - WO + 1) * BLOCK]
                    else:
                        src = w_q[1, :, (i - WQ1) * BLOCK:(i - WQ1 + 1) * BLOCK]
                    if n >= 2:
                        sp.wait_ge(w_used, n - 1)
                    sp.dma_start(wt[:, n % 2], src.rearrange("(k p) n -> p k n", p=P)).then_inc(w_in[n % 2], 16)

            def next_gain(e, n):
                sp.wait_ge(normed, e)
                sp.dma_start(gain[:, :], gains[n:n + 1, :].to_broadcast([P, D])).then_inc(gain_in, 16)

            def load_keys(phase, ready, count):
                sp.wait_ge(ready, count)
                sp.dma_start(topk_in[phase].keysT, keys[phase // NC]).then_inc(keys_in, 16)

            weights(0, 0, 0, 2)
            next_gain(1, 1)
            load_keys(0, y_ready, 1)
            weights(0, 0, 2, 8)
            next_gain(2, 0)
            weights(0, 1, 0, 2)
            next_gain(3, 1)
            weights(0, 1, 2, 5)
            load_keys(1, glu_done, 2)
            weights(0, 1, 5, 8)
            for c in range(NC):
                next_gain(4 + 2 * c, 2)
                weights(1, c, 0, 2)
                next_gain(5 + 2 * c, 3)
                sp.wait_ge(idx_ready, 2 + c)
                n = NG * P * (c + 1)
                sp.dma_start(mask[:, 0:n], masks[:, M_AT[c]:M_AT[c] + n]).then_inc(mask_in, 16)
                weights(1, c, 2, WO + 1)
                load_keys(2 + c, o_turned, c + 1)
                weights(1, c, WO + 1, ITEMS1)
            next_gain(8, 4)
            for c in range(NC):
                sp.wait_ge(out_ready, c + 1)
                sp.dma_start(out[c * P:(c + 1) * P, :], H[:, c, :]).then_inc(out_done, 16)
            sp.wait_ge(out_done, 16 * NC)

        @block.tensor
        def _(pe):
            def pair(r, b, phase, _, first, final):
                pe.wait_ge(diag_ready, b * SETS + (r + 1))
                if first and phase:
                    pe.wait_ge(peer_done, phase)
                for n in range(2):
                    last = pe.matmul(ps[:, n, :], diag[:, r, :],
                                     ring[:, 2 * r, D + n * 512:D + (n + 1) * 512], start=first,
                                     stop=final, skip_group_check=True)
                last.then_inc(v_pe, 1)

            g = Gather(pe, pair)

            def turn(src, event):
                pe.wait_ge(normed, event + 1)
                for k in range(KT):
                    last = pe.transpose(ps[:, 2 + k // 4, (k % 4) * P:(k % 4 + 1) * P],
                                        src[:, k * P:(k + 1) * P], ident)
                last.then_inc(turned, 1)

            def project(n, bank, act):
                pe.wait_ge(w_in[n % 2], 16 * (n // 2 + 1))
                for k in range(KT):
                    last = pe.matmul(ps[:, bank, :], act[:, k, :], wt[:, n % 2, k, :], start=(k == 0),
                                     stop=(k == KT - 1))
                last.then_inc(w_used, 1)

            def project_turned(n, bank):
                pe.wait_ge(w_in[n % 2], 16 * (n // 2 + 1))
                for k in range(KT):
                    for m in range(4):
                        last = pe.matmul(ps[:, bank, m * P:(m + 1) * P], wt[:, n % 2, k, m * P:(m + 1) * P],
                                         hT[:, k, :], start=(k == 0 and m == 0), stop=(k == KT - 1),
                                         skip_group_check=True)
                last.then_inc(w_used, 1)

            def peer_scores(gphase, layer, c, at_norm, at_wq, at_score):
                e, ph = norm_event(layer, c, 1), NC * layer + c
                t = topk_in[ph]
                g.at(gphase, at_norm + 2)
                turn(H[:, c, :], e)
                for i in range(4):
                    g.at(gphase, at_wq + i)
                    if i == 0:
                        pe.wait_ge(hT_ready, e + 1)
                    project_turned(item(layer, c, (WQ0, WQ1)[layer] + i), 4 + i)
                g.at(gphase, at_score)
                pe.wait_ge(q_copied, ph + 1)
                pe.wait_ge(keys_in, 16 * (ph + 1))
                for hp in range(HP):
                    last = pe.matmul(ps[:, 4 + hp // 4, (hp % 4) * P:(hp % 4 + 1) * P], t.qT[:, hp, :],
                                     t.keysT[:, hp, :], start=True, stop=True, skip_group_check=True)
                last.then_inc(score_done, 1)

            def s5_bu(c, k):
                u = KT * c + k
                if k >= 1:
                    pe.wait_ge(bu_used, u)
                for q in range(PPT):
                    rows = slice(32 * q, 32 * (q + 1))
                    for r in range(2):
                        last = pe.matmul(ps[:, 4 + q, r * P:(r + 1) * P], WB[rows, k, r, :],
                                         hT[rows, k, :], start=True, stop=True, skip_group_check=True)
                last.then_inc(bu_ready, 1)

            def s5_y(c, k):
                u = KT * c + k
                pe.wait_ge(prod_ready, u + 1)
                if k == 0 and c == 0:
                    pe.wait_ge(cw_ready, 6)
                if k >= 2:
                    pe.wait_ge(y_skip, u - 1)
                m1, m2, m3, m4 = M[k % 2]
                for q in range(PPT):
                    for i, (w, m) in enumerate(((0, m1), (1, m3), (2, m2), (2, m4))):
                        last = pe.matmul(ps[32 * q:32 * (q + 1), 2 + k % 2, 0:P],
                                         CW[:, PPT * k + q, w, :], m[:, q, :], start=(i == 0),
                                         stop=(i == 3))
                last.then_inc(y_ready, 1)

            def layer0(gphase, c):
                e = norm_event(0, c, 0)
                turn(H[:, c, :], e)
                g.at(gphase, 1)
                pe.wait_ge(hT_ready, e + 1)
                if c == 0:
                    pe.wait_ge(wb_in, 16 * 2 * KT)
                s5_bu(c, 0)
                for k in range(KT):
                    g.at(gphase, S5_K * (k + 1))
                    if k + 1 < KT:
                        s5_bu(c, k + 1)
                    s5_y(c, k)
                for i in range(4):
                    g.at(gphase, GLU_AT + i)
                    if i == 0:
                        pe.wait_ge(y_gelu, KT * (c + 1))
                    project(item(0, c, GLU + i), 4 + i, gT)
                peer_scores(gphase, 0, c, NORM1_AT, WQ_AT, SCORE_AT)

            def attn_turn(n):
                m = 2 * (n // 3) + n % 3
                pe.wait_ge(roped, m + 1)
                if m >= 2:
                    pe.wait_ge(qk_copied, m - 1)
                for j in range(4):
                    last = pe.transpose(ps[:, 4 + m % 2, j * P:(j + 1) * P],
                                        RR[m % 2][:, j * P:(j + 1) * P], ident)
                last.then_inc(qk_turned, 1)

            def attn_s(c, half, h):
                u = HEADS * c + NH * half + h
                rows = slice(DH * (h % 2), DH * (h % 2 + 1))
                if h >= 2 - c:
                    pe.wait_ge(s_masked, u - 1 + c)
                for gr in range(NG):
                    for kb in range(c + 1):
                        at = (1 - c) * 512 * (u % 2) + (gr * (c + 1) + kb) * P
                        kt = K0[rows, gr, 4 * half + h // 2, :] if kb == 0 else K1[rows, gr, h // 2, :]
                        last = pe.matmul(ps[:, 2 + at // 512, at % 512:at % 512 + P],
                                         QT[rows, gr, h // 2, :], kt, start=True, stop=True,
                                         skip_group_check=True)
                last.then_inc(s_done, 1)

            def attn_pt(c, half, h):
                u = HEADS * c + NH * half + h
                pe.wait_ge(p_ready, u + 1)
                if u:
                    pe.wait_ge(pT_copied, u)
                for j in range(NG * (c + 1)):
                    last = pe.transpose(ps[:, 5 + j // 4, (j % 4) * P:(j % 4 + 1) * P],
                                        SS[u % 2][:, j * P:(j + 1) * P], ident)
                last.then_inc(p_turned, 1)

            def attn_pv(c, half, h):
                u = HEADS * c + NH * half + h
                pe.wait_ge(pT_copied, u + 1)
                if h == 0 and u:
                    pe.wait_ge(o_scaled, 2 * c + half)
                n = NG * (c + 1)
                for j in range(n):
                    gr, kb = divmod(j, c + 1)
                    vv = (V0[:, gr, (NH * half + h) * DH:(NH * half + h + 1) * DH] if kb == 0 else
                          V1[:, gr, h * DH:(h + 1) * DH])
                    last = pe.matmul(ps[:, 7, h * DH:(h + 1) * DH], PT[u % 2][:, j * P:(j + 1) * P], vv,
                                     start=(j == 0), stop=(j == n - 1), skip_group_check=True)
                last.then_inc(pv_done, 1)

            def layer1(gphase, c):
                e = norm_event(1, c, 0)
                g.at(gphase, 3)
                turn(H[:, c, :], e)
                for half in range(2):
                    base = A_QKV + A_HALF * half
                    for j in range(11):
                        g.at(gphase, base + j)
                        n = 9 * (2 * c + half) + j
                        if j < 9:
                            if j == 0 and half == 0:
                                pe.wait_ge(hT_ready, e + 1)
                            if j == 0 and half == 1:
                                pe.wait_ge(s_masked, HEADS * c + NH)
                            if j >= 2:
                                pe.wait_ge(acc_evac, n - 1)
                            project(item(1, c, QKV + 9 * half + j), 2 + j % 2, hT)
                        if j >= 2 and (j - 2) % 3 < 2:
                            attn_turn(n - 2)
                    base = A_HEADS + A_HALF * half
                    for i in range(NH + 3):
                        g.at(gphase, base + 1 + i)
                        if i == 0:
                            pe.wait_ge(qk_copied, 6 * (2 * c + half + 1))
                            pe.wait_ge(acc_evac, 9 * (2 * c + half + 1))
                        if 2 <= i < NH + 2:
                            attn_pt(c, half, i - 2)
                        if i >= 3:
                            attn_pv(c, half, i - 3)
                        if i < NH:
                            attn_s(c, half, i)
                g.at(gphase, A_WO)
                pe.wait_ge(o_scaled, 2 * (c + 1))
                for k in range(KT):
                    last = pe.transpose(ps[:, 2 + k // 4, (k % 4) * P:(k % 4 + 1) * P],
                                        O[:, k * P:(k + 1) * P], ident)
                last.then_inc(o_turned, 1)
                for i in range(2):
                    g.at(gphase, A_WO + 1 + i)
                    if i == 0:
                        pe.wait_ge(oT_ready, c + 1)
                    project(item(1, c, WO + i), 4 + i, gT)
                peer_scores(gphase, 1, c, A_NORM, A_WQ, A_SCORE)

            pe.wait_ge(con_in, 16)
            layer0(None, 0)
            layer0(0, 1)
            g.at(0, PAIRS_G)
            layer1(1, 0)
            g.at(1, PAIRS_G)
            layer1(2, 1)
            g.at(2, PAIRS_G)
            g.at(3, PAIRS_G)

        @block.scalar
        def _(act):
            steps = [0]

            def link(ins):
                steps[0] += 1
                ins.then_inc(act_step, 1)
                act.wait_ge(act_step, steps[0])

            def pair(r, b, phase, _, first, final):
                act.wait_ge(dots_ready, b * SETS + (r + 1))
                act.activation(gelus[:, 2 * r:2 * r + 2], dots[:, 2 * r:2 * r + 2],
                               ACT.Gelu_apprx_tanh).then_inc(gelu_ready, 1)
                act.wait_ge(wts_ready, b * SETS + (r + 1))
                act.activation(diag[:, r, :], ident, ACT.Copy,
                               scale=wts[:, 2 * r:2 * r + 1]).then_inc(diag_ready, 1)

            g = Gather(act, pair)

            def root(e):
                act.wait_ge(var_ready, e + 1)
                act.activation(stat[:, 2:3], stat[:, 1:2], ACT.Sqrt).then_inc(root_ready, 1)

            def copy_turn(dst, src_ready, count, done):
                act.wait_ge(src_ready, count)
                act.copy(dst[:, :, :].rearrange("p k t -> p (k t)"), banks(2, 4)).then_inc(done, 1)

            def peer_scores(gphase, layer, c, at_norm, at_wq, at_score, at_topk):
                e, ph = norm_event(layer, c, 1), NC * layer + c
                t = topk_in[ph]
                g.at(gphase, at_norm + 1)
                root(e)
                g.at(gphase, at_norm + 3)
                copy_turn(hT, turned, e + 1, hT_ready)
                g.at(gphase, at_wq + 4)
                act.wait_ge(w_used, item(layer, c, (WQ0, WQ1)[layer] + 4))
                act.copy(t.qT.rearrange("p k t -> p (k t)"), banks(4, 8)).then_inc(q_copied, 1)
                g.at(gphase, at_score + 1)
                act.wait_ge(score_done, ph + 1)
                act.copy(t.S.rearrange("p k t -> p (k t)"), banks(4, 8)).then_inc(score_copied, 1)
                g.at(gphase, at_topk + 10)
                act.wait_ge(best_ready, ph + 1)
                act.activation(gate[:, c, :], gate[:, c, :], ACT.Exp).then_inc(gate_exp, 1)

            def layer0(gphase, c):
                e = norm_event(0, c, 0)
                root(e)
                g.at(gphase, 1)
                copy_turn(hT, turned, e + 1, hT_ready)
                if c == 0:
                    for k in range(KT):
                        q = slice(PPT * k, PPT * (k + 1))
                        act.wait_ge(tab_dve, k + 1)
                        link(act.activation(cosT[:, q, :], sinT[:, q, :], ACT.Abs))
                        act.activation(cosT[:, q, :], cosT[:, q, :], ACT.Sin, bias=half_pi[:, 0:1], scale=-TWO_PI)
                        act.activation(sinT[:, q, :], sinT[:, q, :], ACT.Sin, scale=TWO_PI).then_inc(tab_act, 1)
                for k in range(KT):
                    g.at(gphase, S5_K * (k + 1) + 1)
                    act.wait_ge(y_skip, KT * c + k + 1)
                    act.activation(gT[:, k, :], gT[:, k, :], ACT.Gelu_apprx_tanh).then_inc(y_gelu, 1)
                g.at(gphase, GLU_AT + 4)
                act.wait_ge(w_used, item(0, c, GLU + 4))
                act.activation(sig, banks(6, 8), ACT.Sigmoid).then_inc(sig_ready, 1)
                peer_scores(gphase, 0, c, NORM1_AT, WQ_AT, SCORE_AT, TOPK_AT)

            def exp_p(c, half, h):
                u, n = HEADS * c + NH * half + h, NG * P * (c + 1)
                act.wait_ge(nmx_ready, u + 1)
                act.activation(SS[u % 2][:, 0:n], SS[u % 2][:, 0:n], ACT.Exp, bias=nmx[:, u:u + 1],
                               scale=DH ** -0.5, accum_out=den[:, u:u + 1]).then_inc(p_ready, 1)

            def copy_pt(c, half, h):
                u, n = HEADS * c + NH * half + h, NG * P * (c + 1)
                act.wait_ge(p_turned, u + 1)
                if u >= 2:
                    act.wait_ge(pv_done, u - 1)
                act.copy(PT[u % 2][:, 0:n], banks(5, 7)[:, 0:n]).then_inc(pT_copied, 1)

            def layer1(gphase, c):
                e = norm_event(1, c, 0)
                g.at(gphase, 1)
                root(e)
                g.at(gphase, 4)
                copy_turn(hT, turned, e + 1, hT_ready)
                for half in range(2):
                    base = A_QKV + A_HALF * half
                    for j in range(9 + 3):
                        g.at(gphase, base + j)
                        if j >= 1 and j <= 9 and (j - 1) % 3 == 2:
                            act.wait_ge(w_used, item(1, c, QKV + 9 * half + j))
                            gr = (j - 1) // 3
                            dst = V0[:, gr, half * BLOCK:(half + 1) * BLOCK] if c == 0 else V1[:, gr, :]
                            act.copy(dst, ps[:, 2 + (j - 1) % 2, :]).then_inc(acc_evac, 1)
                        if j >= 3 and (j - 3) % 3 < 2:
                            gr, k = divmod(j - 3, 3)
                            m = 6 * (2 * c + half) + 2 * gr + k
                            act.wait_ge(qk_turned, m + 1)
                            dst = (QT[:, gr] if k == 0 else
                                   K0[:, gr, 4 * half:4 * half + 4, :] if c == 0 else K1[:, gr])
                            act.copy(dst.rearrange("p m t -> p (m t)"), ps[:, 4 + m % 2, :]).then_inc(qk_copied, 1)
                    base = A_HEADS + A_HALF * half
                    for i in range(1, NH + 3):
                        g.at(gphase, base + 1 + i)
                        if i - 1 < NH:
                            exp_p(c, half, i - 1)
                        if i >= 3:
                            copy_pt(c, half, i - 3)
                g.at(gphase, A_WO + 1)
                copy_turn(gT, o_turned, c + 1, oT_ready)
                peer_scores(gphase, 1, c, A_NORM, A_WQ, A_SCORE, A_TOPK_AT)

            act.wait_ge(lam_in, 32)
            act.activation(step, small[:, 2, :], ACT.Exp).then_inc(lam_act, 1)
            act.wait_ge(lam_dve, 1)
            act.activation(mag, xr, ACT.Exp).then_inc(lam_act, 1)
            act.wait_ge(lam_dve, 2)
            act.activation(sn, frac, ACT.Sin, scale=TWO_PI).then_inc(lam_act, 1)
            act.wait_ge(zeroed, 3)
            link(act.activation(absf, frac, ACT.Abs))
            act.activation(cs, absf, ACT.Sin, bias=half_pi[:, 0:1], scale=-TWO_PI).then_inc(lam_act, 1)
            layer0(None, 0)
            layer0(0, 1)
            g.at(0, PAIRS_G)
            layer1(1, 0)
            g.at(1, PAIRS_G)
            layer1(2, 1)
            g.at(2, PAIRS_G)
            g.at(3, 2)
            root(8)
            g.at(3, PAIRS_G)
            root(9)

        @block.gpsimd
        def _(pool):
            pool.memset(WB.rearrange("p a b c -> p (a b c)"), 0.0).then_inc(zeroed, 1)
            pool.memset(CW.rearrange("p a b c -> p (a b c)"), 0.0).then_inc(zeroed, 1)
            pool.memset(half_pi[:, :], HALF_PI).then_inc(zeroed, 1)

            def pair(phase, b, r, first):
                c = phase % NC
                if not first:
                    pool.wait_ge(v_pe, b * SETS + (phase * PAIRS_G + r - SETS + 1))
                    pool.wait_ge(v_dve, b * SETS + (phase * PAIRS_G + r - SETS + 1))
                at = bass.ds(b * RING + 2 * r, 2)
                pool.tensor_tensor(rows_now[:, r, :], row_a[:, c, at], row_b[:, c, at],
                                   ALU.add).then_inc(rows_ready, 1)
                pool.wait_ge(rows_ready, b * SETS + (phase * PAIRS_G + r + 1))
                pool.tensor_tensor(tick[:, :], rows_now[:, r, 0:1], rows_now[:, r, 0:1], ALU.add)
                for i in range(2):
                    pool.indirect_dma_start(
                        ring[:, 2 * r + i, :], None, experts[phase // NC],
                        bass.IndirectOffsetOnAxis(ap=rows_now[:, r, i:i + 1], axis=0)
                    ).then_inc(landed[2 * r + i], 16)

            for phase in range(2 * NC):
                pool.wait_ge(idx_ready, phase + 1)
                for r in range(SETS):
                    pair(phase, 0, r, first=(phase == 0))
                with pool.Fori(1, ROUNDS) as b:
                    for r in range(SETS):
                        pair(phase, b, r, first=False)

        @block.vector
        def _(v):
            steps = [0]

            def link(ins):
                steps[0] += 1
                ins.then_inc(dve, 1)
                v.wait_ge(dve, steps[0])

            def pair(r, b, phase, bp, first, final):
                c = phase % NC
                for i in (2 * r, 2 * r + 1):
                    v.wait_ge(landed[i], b * 16 + 16)
                    last = v.tensor_tensor_reduce(ring[:, i, 0:D], ring[:, i, 0:D], H[:, c, :],
                                                  1.0, 0.0, ALU.mult, ALU.add, dots[:, i:i + 1])
                last.then_inc(dots_ready, 1)
                v.wait_ge(gelu_ready, b * SETS + (r + 1))
                v.tensor_tensor(wts[:, 2 * r:2 * r + 2], gelus[:, 2 * r:2 * r + 2],
                                gate[:, c, bass.ds(bp * RING + 2 * r, 2)], ALU.mult).then_inc(wts_ready, 1)
                v.wait_ge(wts_ready, b * SETS + (r + 1))
                if not (first and phase == 0):
                    v.wait_ge(v_dve, b * SETS + r)
                v.scalar_tensor_tensor(out=X[:, c, :], in0=ring[:, 2 * r + 1, D:2 * D],
                                       scalar=wts[:, 2 * r + 1:2 * r + 2], in1=X[:, c, :],
                                       op0=ALU.mult, op1=ALU.add).then_inc(v_dve, 1)

            g = Gather(v, pair)

            def peer_end(phase):
                c = phase % NC
                g.at(phase, PAIRS_G)
                v.wait_ge(v_pe, PAIRS_G * (phase + 1))
                v.wait_ge(v_dve, PAIRS_G * (phase + 1))
                v.tensor_tensor(X[:, c, :], X[:, c, :], banks(0, 2), ALU.add).then_inc(peer_done, 1)

            def norm(gphase, start, c, e, done, count):
                link(v.tensor_tensor_reduce(H[:, c, :], X[:, c, :], X[:, c, :], 1.0, 0.0, ALU.mult,
                                            ALU.add, stat[:, 0:1]))
                v.tensor_scalar(stat[:, 1:2], stat[:, 0:1], 1.0 / D, EPS, ALU.mult,
                                ALU.add).then_inc(var_ready, 1)
                g.at(gphase, start + 1)
                v.wait_ge(root_ready, e + 1)
                link(v.reciprocal(stat[:, 3:4], stat[:, 2:3]))
                v.wait_ge(gain_in, 16 * (min(e, 8) + 1))
                v.scalar_tensor_tensor(out=H[:, c, :], in0=X[:, c, :], scalar=stat[:, 3:4],
                                       in1=gain[:, :], op0=ALU.mult, op1=ALU.mult).then_inc(done, 1)

            def s5_lambda():
                v.wait_ge(lam_in, 32)
                v.wait_ge(lam_act, 1)
                v.tensor_tensor(xr, lre, step, ALU.mult).then_inc(lam_dve, 1)
                link(v.tensor_tensor(turn, lim, step, ALU.mult))
                link(v.tensor_scalar(turn, turn, 1.0 / (2.0 * np.pi), None, ALU.mult))
                link(v.tensor_scalar(whole, turn, ROUND, -ROUND, ALU.add, ALU.add))
                v.tensor_tensor(frac, turn, whole, ALU.subtract).then_inc(lam_dve, 1)
                v.wait_ge(lam_dve, 2)

            def s5_tables():
                v.wait_ge(con_in, 16)
                for k in range(KT):
                    q = slice(PPT * k, PPT * (k + 1))
                    shape = [P, PPT, P]
                    link(v.tensor_tensor(sinT[:, q, :], spread(ramp, 1, shape),
                                         spread(frac[:, q], 2, shape), ALU.mult))
                    link(v.tensor_scalar(cosT[:, q, :], sinT[:, q, :], ROUND, -ROUND, ALU.add, ALU.add))
                    v.tensor_tensor(sinT[:, q, :], sinT[:, q, :], cosT[:, q, :],
                                    ALU.subtract).then_inc(tab_dve, 1)

            def s5_coef():
                v.wait_ge(lam_act, 4)
                v.tensor_tensor(lbim, mag, sn, ALU.mult)
                v.tensor_tensor(ta, lre, lre, ALU.mult)
                v.tensor_tensor(tb, lim, lim, ALU.mult)
                link(v.tensor_tensor(lbre, mag, cs, ALU.mult))
                v.tensor_tensor(dn, ta, tb, ALU.add)
                link(v.tensor_scalar(lbre, lbre, -1.0, None, ALU.add))
                v.reciprocal(rdn, dn)
                v.tensor_tensor(ta, lbre, lre, ALU.mult)
                link(v.tensor_tensor(tb, lbim, lim, ALU.mult))
                link(v.tensor_tensor(cre, ta, tb, ALU.add))
                v.tensor_tensor(cre, cre, rdn, ALU.mult)
                v.tensor_tensor(ta, lbim, lre, ALU.mult)
                link(v.tensor_tensor(tb, lbre, lim, ALU.mult))
                link(v.tensor_tensor(cim, ta, tb, ALU.subtract))
                link(v.tensor_tensor(cim, cim, rdn, ALU.mult))
                v.wait_ge(craw_in, 16)
                v.wait_ge(zeroed, 3)
                shape = [P, PAIRS, GH]
                re, im = spread(cre, 2, shape), spread(cim, 2, shape)
                v.tensor_tensor(tmpc[:, 0], craw[:, 0], re, ALU.mult)
                link(v.tensor_tensor(tmpc[:, 1], craw[:, 1], im, ALU.mult))
                link(v.tensor_tensor(tmpc[:, 0], tmpc[:, 0], tmpc[:, 1], ALU.subtract))
                for a in range(2):
                    half = slice(STATE * a, STATE * (a + 1))
                    cols = slice(GH * a, GH * (a + 1))
                    v.tensor_copy(CW[half, :, 0, cols], tmpc[half, 0]).then_inc(cw_ready, 1)
                    v.tensor_scalar(CW[half, :, 1, cols], tmpc[half, 0], -1.0, None,
                                    ALU.mult).then_inc(cw_ready, 1)
                v.wait_ge(cw_ready, 4)
                v.tensor_tensor(tmpc[:, 0], craw[:, 0], im, ALU.mult)
                link(v.tensor_tensor(tmpc[:, 1], craw[:, 1], re, ALU.mult))
                link(v.tensor_tensor(tmpc[:, 0], tmpc[:, 0], tmpc[:, 1], ALU.add))
                for a in range(2):
                    half = slice(STATE * a, STATE * (a + 1))
                    cols = slice(GH * a, GH * (a + 1))
                    v.tensor_scalar(CW[half, :, 2, cols], tmpc[half, 0], -1.0, None,
                                    ALU.mult).then_inc(cw_ready, 1)

            def tile_of(t, k):
                return t[:, PPT * k:PPT * (k + 1), :]

            def s5_rotate(c, k):
                m1, m2, m3, m4 = M[k % 2]
                u = KT * c + k
                v.wait_ge(bu_ready, u + 1)
                v.wait_ge(tab_act, k + 1)
                if u >= 2:
                    v.wait_ge(y_ready, u - 1)
                co, si = tile_of(cosT, k), tile_of(sinT, k)
                bre, bim = ps[:, 4:8, 0:P], ps[:, 4:8, P:2 * P]
                v.tensor_tensor(m1, co, bre, ALU.mult)
                v.tensor_tensor(m2, si, bim, ALU.mult)
                v.tensor_tensor(m3, co, bim, ALU.mult)
                v.tensor_tensor(m4, si, bre, ALU.mult).then_inc(bu_used, 1)
                v.wait_ge(bu_used, u + 1)
                v.tensor_tensor(m1, m1, m2, ALU.add)
                link(v.tensor_tensor(m3, m3, m4, ALU.subtract))

            def s5_scan(c, k):
                m1, m2, m3, m4 = M[k % 2]
                u = KT * c + k
                for src, dst, z0 in ((m1, m2, z0re), (m3, m4, z0im)):
                    for q in range(PPT):
                        n = PPT * k + q
                        last = v.tensor_tensor_scan(dst[:, q, :], mag[:, n:n + 1].to_broadcast([P, P]),
                                                    src[:, q, :], z0[:, n:n + 1] if c else 0.0,
                                                    ALU.mult, ALU.add)
                link(last)
                co, si, q = tile_of(cosT, k), tile_of(sinT, k), slice(PPT * k, PPT * (k + 1))
                if c == 0:
                    end = slice(P - 1, P)
                    def col(t):
                        return t[:, q].unsqueeze(2)
                    v.tensor_tensor(col(z0re), co[:, :, end], m2[:, :, end], ALU.mult)
                    v.tensor_tensor(col(zta), si[:, :, end], m4[:, :, end], ALU.mult)
                    v.tensor_tensor(col(z0im), si[:, :, end], m2[:, :, end], ALU.mult)
                    link(v.tensor_tensor(col(ztb), co[:, :, end], m4[:, :, end], ALU.mult))
                    v.tensor_tensor(z0re[:, q], z0re[:, q], zta[:, q], ALU.subtract)
                    link(v.tensor_tensor(z0im[:, q], z0im[:, q], ztb[:, q], ALU.add))
                v.tensor_tensor(m1, co, m2, ALU.mult)
                v.tensor_tensor(m3, si, m4, ALU.mult)
                v.tensor_tensor(m2, si, m2, ALU.mult)
                v.tensor_tensor(m4, co, m4, ALU.mult).then_inc(prod_ready, 1)

            def s5_skip(c, k):
                v.wait_ge(y_ready, KT * c + k + 1)
                v.scalar_tensor_tensor(out=gT[:, k, :], in0=hT[:, k, :], scalar=skip[:, k:k + 1],
                                       in1=ps[:, 2 + k % 2, 0:P], op0=ALU.mult,
                                       op1=ALU.add).then_inc(y_skip, 1)

            def layer0(gphase, c):
                if c == 0:
                    s5_tables()
                    s5_coef()
                for k in range(KT):
                    if k == 0:
                        g.at(gphase, 1)
                        s5_rotate(c, 0)
                    g.at(gphase, S5_K * k + 2)
                    s5_scan(c, k)
                    g.at(gphase, S5_K * (k + 1) + 1)
                    if k + 1 < KT:
                        s5_rotate(c, k + 1)
                    s5_skip(c, k)
                g.at(gphase, GLU_AT + 5)
                v.wait_ge(sig_ready, c + 1)
                link(v.tensor_tensor(sig, sig, banks(4, 6), ALU.mult))
                v.tensor_tensor(X[:, c, :], X[:, c, :], sig, ALU.add).then_inc(glu_done, 1)
                v.wait_ge(glu_done, c + 1)
                norm(gphase, NORM1_AT, c, norm_event(0, c, 1), normed, 0)
                top_k(gphase, 0, c, TOPK_AT)

            def top_k(gphase, layer, c, start):
                ph = NC * layer + c
                t = topk_in[ph]
                stop, itop, best, pos = t.stop, t.itop, t.best, t.pos
                g.at(gphase, start)
                v.wait_ge(score_copied, ph + 1)
                for hp in range(HP):
                    last = v.max(stop[:, hp, 0:8], t.S[:, hp, :])
                link(last)
                for hp in range(HP):
                    if hp % 8 == 0:
                        g.at(gphase, start + 1 + hp // 8)
                    v.match_replace(t.S2[:, hp, :], stop[:, hp, 0:8], t.S[:, hp, :], NEG)
                    last = v.max_index(itop[:, hp, 0:8], stop[:, hp, 0:8], t.S[:, hp, :])
                link(last)
                g.at(gphase, start + 3)
                for hp in range(HP):
                    last = v.max(stop[:, hp, 8:16], t.S2[:, hp, :])
                link(last)
                g.at(gphase, start + 4)
                for hp in range(HP):
                    last = v.max_index(itop[:, hp, 8:16], stop[:, hp, 8:16], t.S2[:, hp, :])
                link(last)
                g.at(gphase, start + 5)
                halves = stop.rearrange("p (h two) k -> p h two k", two=2)
                ihalves = t.itopf.rearrange("p (h two) k -> p h two k", two=2)
                v.tensor_copy(t.itopf, itop)
                shape = [P, PH, TOPK, TOPK]
                cand4 = t.S.rearrange("p (h two) (i j) -> p h (two i) j", two=2, j=TOPK)
                link(v.tensor_tensor(cand4, spread(halves[:, :, 0, :], 3, shape),
                                     spread(halves[:, :, 1, :], 2, shape), ALU.add))
                ca = t.S.rearrange("p (h two) n -> p h (two n)", two=2)
                cb = t.S2.rearrange("p (h two) n -> p h (two n)", two=2)
                for h in range(PH):
                    last = v.max(best[:, h, 0:8], ca[:, h, :])
                link(last)
                g.at(gphase, start + 6)
                for h in range(PH):
                    v.match_replace(cb[:, h, :], best[:, h, 0:8], ca[:, h, :], NEG)
                    last = v.max_index(pos[:, h, 0:8], best[:, h, 0:8], ca[:, h, :])
                link(last)
                g.at(gphase, start + 7)
                for h in range(PH):
                    last = v.max(best[:, h, 8:16], cb[:, h, :])
                link(last)
                g.at(gphase, start + 8)
                for h in range(PH):
                    last = v.max_index(pos[:, h, 8:16], best[:, h, 8:16], cb[:, h, :])
                link(last)
                g.at(gphase, start + 9)
                g3 = gate[:, c, :].rearrange("p (h k) -> p h k", h=PH)
                v.tensor_tensor(g3, best, best[:, :, 0:1].to_broadcast([P, PH, TOPK]),
                                ALU.subtract).then_inc(best_ready, 1)
                v.tensor_scalar(t.posi, pos, 4, None, ALU.logical_shift_right)
                link(v.tensor_scalar(t.posj, pos, TOPK - 1, None, ALU.bitwise_and))
                v.tensor_copy(t.posif, t.posi)
                link(v.tensor_copy(t.posjf, t.posj))
                for src, half in ((t.posjf, 1), (t.posif, 0)):
                    shape = [P, STEPS, TOPK]
                    link(v.tensor_tensor(t.EQ, spread(src.rearrange("p h k -> p (h k)"), 2, shape),
                                         spread(iota, 1, shape), ALU.is_equal))
                    eq4 = t.EQ.rearrange("p (h k) i -> p h k i", h=PH)
                    link(v.tensor_tensor(eq4, eq4, spread(ihalves[:, :, half, :], 2,
                                                          [P, PH, TOPK, TOPK]), ALU.mult))
                    link(v.tensor_reduce(t.keyf, t.EQ, AX.X, ALU.add))
                    if half:
                        link(v.tensor_copy(row_b[:, c, :], t.keyf))
                        g.at(gphase, start + 10)
                link(v.tensor_scalar(row_a[:, c, :], t.keyf, float(NKEYS), None, ALU.mult))
                g.at(gphase, start + 11)
                v.wait_ge(gate_exp, ph + 1)
                link(v.tensor_reduce(t.gsum, g3, AX.X, ALU.add))
                link(v.reciprocal(t.grec, t.gsum))
                v.tensor_tensor(g3, g3, spread(t.grec, 2, [P, PH, TOPK]), ALU.mult).then_inc(idx_ready, 1)
                v.wait_ge(idx_ready, ph + 1)

            def rope(c, half, j):
                n = 9 * (2 * c + half) + j
                m = 2 * (n // 3) + n % 3
                v.wait_ge(w_used, item(1, c, QKV + 9 * half + j) + 1)
                shape = [P, NH, DH]
                acc, ra, rb, rr = [t.rearrange("p (h e) -> p h e", h=NH)
                                   for t in (ps[:, 2 + j % 2, :], RA, RB, RR[m % 2])]
                cos = con[:, C_COS + DH * c:C_COS + DH * (c + 1)]
                sin = con[:, C_SIN + DH * c:C_SIN + DH * (c + 1)]
                v.tensor_tensor(ra, acc, spread(cos, 1, shape), ALU.mult)
                v.tensor_tensor(rb, acc, spread(sin, 1, shape), ALU.mult).then_inc(acc_evac, 1)
                v.wait_ge(acc_evac, n + 1)
                if m >= 2:
                    v.wait_ge(qk_turned, m - 1)
                lo, hi = slice(0, DH // 2), slice(DH // 2, DH)
                v.tensor_tensor(rr[:, :, lo], ra[:, :, lo], rb[:, :, hi], ALU.subtract)
                v.tensor_tensor(rr[:, :, hi], ra[:, :, hi], rb[:, :, lo], ALU.add).then_inc(roped, 1)

            def attn_mask(c, half, h):
                u, n = HEADS * c + NH * half + h, NG * P * (c + 1)
                v.wait_ge(s_done, u + 1)
                if u >= 2:
                    v.wait_ge(p_turned, u - 1)
                at = (1 - c) * 512 * (u % 2)
                v.tensor_tensor_reduce(SS[u % 2][:, 0:n], banks(2, 4)[:, at:at + n], mask[:, 0:n],
                                       1.0, NEG, ALU.add, ALU.max, mx[:, u:u + 1]).then_inc(s_masked, 1)
                v.wait_ge(s_masked, u + 1)
                v.tensor_scalar(nmx[:, u:u + 1], mx[:, u:u + 1], -(DH ** -0.5), None,
                                ALU.mult).then_inc(nmx_ready, 1)

            def attn_scale(c, half):
                u = HEADS * c + NH * half
                v.wait_ge(pv_done, u + NH)
                v.wait_ge(p_ready, u + NH)
                link(v.reciprocal(rden[:, u:u + NH], den[:, u:u + NH]))
                v.tensor_tensor(O[:, half * BLOCK:(half + 1) * BLOCK].rearrange("p (h e) -> p h e", h=NH),
                                ps[:, 7, :].rearrange("p (h e) -> p h e", h=NH),
                                spread(rden[:, u:u + NH], 2, [P, NH, DH]), ALU.mult).then_inc(o_scaled, 1)

            def layer1(gphase, c):
                norm(gphase, 1, c, norm_event(1, c, 0), normed, 0)
                for half in range(2):
                    base = A_QKV + A_HALF * half
                    for j in range(9):
                        g.at(gphase, base + 1 + j)
                        if j % 3 < 2:
                            rope(c, half, j)
                    base = A_HEADS + A_HALF * half
                    if half == 0:
                        v.wait_ge(mask_in, 16 * (c + 1))
                    for i in range(1, NH + 1):
                        g.at(gphase, base + 1 + i)
                        attn_mask(c, half, i - 1)
                    g.at(gphase, base + 1 + NH + 3)
                    attn_scale(c, half)
                g.at(gphase, A_WO + 3)
                v.wait_ge(w_used, item(1, c, WO + 2))
                v.tensor_tensor(X[:, c, :], X[:, c, :], banks(4, 6), ALU.add).then_inc(wo_done, 1)
                v.wait_ge(wo_done, c + 1)
                norm(gphase, A_NORM, c, norm_event(1, c, 1), normed, 0)
                top_k(gphase, 1, c, A_TOPK_AT)

            s5_lambda()
            v.wait_ge(x_in[0], 16)
            norm(None, 0, 0, 0, normed, 0)
            layer0(None, 0)
            v.wait_ge(x_in[1], 16)
            norm(None, 0, 1, norm_event(0, 1, 0), normed, 0)
            layer0(0, 1)
            peer_end(0)
            v.wait_ge(peer_done, 1)
            layer1(1, 0)
            peer_end(1)
            v.wait_ge(peer_done, 2)
            layer1(2, 1)
            peer_end(2)
            v.wait_ge(peer_done, 3)
            norm(3, 2, 0, 8, out_ready, 0)
            peer_end(3)
            v.wait_ge(peer_done, 4)
            norm(None, 0, 1, 9, out_ready, 0)


def _constants():
    con = np.zeros((P, C_ALL), np.float32)
    con[:, C_ID:C_ID + P] = np.eye(P)
    con[:, C_RAMP:C_RAMP + P] = np.arange(1, P + 1)
    con[:, C_IOTA:C_IOTA + TOPK] = np.arange(TOPK)
    inv = np.float32(10000.0) ** (-np.arange(DH // 2, dtype=np.float32) / np.float32(DH // 2))
    ang = np.arange(SEQ, dtype=np.float32)[:, None] * inv.astype(np.float32)[None, :]
    for c in range(NC):
        a = np.tile(ang[c * P:(c + 1) * P], (1, 2))
        con[:, C_COS + DH * c:C_COS + DH * (c + 1)] = np.cos(a)
        con[:, C_SIN + DH * c:C_SIN + DH * (c + 1)] = np.sin(a)
    masks = np.zeros((P, M_ALL), np.float32)
    for c in range(NC):
        n = P * (c + 1)
        for g, (window, dilation) in enumerate(DILATED):
            dist = (c * P + np.arange(P))[:, None] - np.arange(n)[None, :]
            seen = (dist >= 0) & (dist <= window) & (dist % dilation == 0)
            masks[:, M_AT[c] + g * n:M_AT[c] + (g + 1) * n] = np.where(seen, 0.0, MASKED)
    return con, masks


def _layout(i):
    con, masks = _constants()
    def by_state(t):
        return t.reshape(PAIRS, 2, STATE).transpose(1, 2, 0).reshape(P, PAIRS)
    step = np.repeat(i["s5_log_step"][0], STATE).reshape(GROUPS, STATE)
    lam = np.stack([by_state(i["s5_lam_re"][0]), by_state(i["s5_lam_im"][0]), by_state(step)], 1)
    b = np.stack([i["s5_b_re"][0], i["s5_b_im"][0]])
    b = b.reshape(2, KT, 8, STATE, GH).transpose(0, 2, 4, 1, 3)
    c = np.stack([i["s5_c_re"][0], i["s5_c_im"][0]])
    c = c.reshape(2, PAIRS, 2, GH, STATE).transpose(2, 4, 0, 1, 3).reshape(P, 2, PAIRS, GH)
    return {
        "x": i["x"].reshape(SEQ, D),
        "gains": np.stack([i["norm_mix"][0], i["norm_ffn"][0], i["norm_mix"][1], i["norm_ffn"][1],
                           i["norm_final"]]),
        "lam": lam, "b_in": b, "c_out": c,
        "d_skip": i["s5_d"][0].reshape(KT, P).T,
        "w_glu": i["s5_w_glu"][0], "w_qkv": i["attn_w_qkv"][0], "w_o": i["attn_w_o"][0],
        "w_q": i["peer_w_q"],
        "keys": i["peer_sub_keys"].reshape(2, HP, NKEYS, P).transpose(0, 3, 1, 2),
        "experts0": np.concatenate([i["peer_u"][0], i["peer_v"][0]], axis=1),
        "experts1": np.concatenate([i["peer_u"][1], i["peer_v"][1]], axis=1),
        "consts": con, "masks": masks,
    }


def kernel(**inputs):
    import concourse.bacc as bacc
    from concourse.bass_utils import run_bass_kernel_spmd

    arrays = {k: np.ascontiguousarray(a) for k, a in
              _layout({k: np.asarray(v) for k, v in inputs.items()}).items()}
    nc = bacc.Bacc("TRN2", target_bir_lowering=False, num_devices=1)
    ap = {k: nc.dram_tensor(k, a.shape, mybir.dt.from_np(a.dtype), kind="ExternalInput").ap()
          for k, a in arrays.items()}
    out = nc.dram_tensor("out", (SEQ, D), F32, kind="ExternalOutput").ap()
    ap["experts"] = [ap.pop("experts0"), ap.pop("experts1")]
    build(nc, out=out, **ap)
    r = run_bass_kernel_spmd(nc, [arrays], core_ids=[0])
    return r.results[0]["out"].reshape(1, SEQ, D)
```

```python
from contextlib import ExitStack

import numpy as np

import concourse.bass as bass
from concourse import mybir

F32 = mybir.dt.float32
U32 = mybir.dt.uint32
ALU = mybir.AluOpType
ACT = mybir.ActivationFunctionType
AX = mybir.AxisListType

P = 128
D = 1024
SEQ = 256
NC = SEQ // P
KT = D // P
EPS = 1e-6
GROUPS, STATE, GH = 64, 64, 16
PAIRS = GROUPS // 2
PPT = PAIRS // KT
HEADS, DH = 16, 64
DILATED = ((128, 1), (512, 4), (2048, 16))
NG = len(DILATED)
PH, NKEYS, TOPK = 8, 128, 16
QUARTERS = 4
QH, QHP = PH // QUARTERS, 2 * PH // QUARTERS
QSTEPS = QH * TOPK
HP = 2 * PH
STEPS = PH * TOPK
RING = 8
SETS = RING // 2
PAIRS_G = STEPS // 2
ROUNDS = STEPS // RING
BLOCK = 512
NH = HEADS // 2
NEG = -3.0e38
MASKED = -8.0e30
TWO_PI = 6.283185
HALF_PI = 1.5707963
ROUND = 12582912.0

GLU, WQ0, ITEMS0 = 0, 4, 8
QKV, WO, WQ1, ITEMS1 = 0, 18, 20, 24

C_ID, C_RAMP, C_IOTA, C_COS, C_SIN, C_ALL = 0, 128, 256, 272, 400, 528
M_AT = (0, NG * P)
M_ALL = NG * P + NG * 2 * P
A_WORDS = 18176


def item(layer, c, i):
    return (ITEMS0 * c if layer == 0 else NC * ITEMS0 + ITEMS1 * c) + i - WQ0


def norm_event(layer, c, ffn):
    return 4 * layer + 2 * c + ffn


SEGMENTS = (0, 8, 12, 44, PAIRS_G)


def both_on_pe(phase, p):
    return p < (44, 8, 8, 0)[phase]


def build(nc, x, gains, lam, b_in, c_out, d_skip, w_glu, w_qkv, w_o, w_q, keys, experts, consts,
          masks, out):
    ctx = ExitStack()
    with ctx:
        def sb(name, shape, dt=F32):
            return ctx.enter_context(nc.sbuf_tensor(name, shape, dt))

        def sem(name):
            return ctx.enter_context(nc.semaphore(name))

        X = sb("X", [P, NC, D])
        H = sb("H", [P, NC, D])
        hT = sb("hT", [P, KT, P])
        gT = sb("gT", [P, KT, P])
        gain = sb("gain", [P, D])
        wt = sb("wt", [P, 2, KT, BLOCK])
        ringmem = sb("ringmem", [P, RING * 2 * D])
        area = sb("area", [P, A_WORDS])
        con = sb("con", [P, C_ALL])
        row_a = sb("row_a", [P, NC, STEPS], U32)
        row_b = sb("row_b", [P, NC, STEPS], U32)
        gate = sb("gate", [P, NC, STEPS])
        rows_now = sb("rows_now", [P, SETS, 2], U32)
        tick = sb("tick", [P, 1], U32)
        dots = sb("dots", [P, RING])
        gelus = sb("gelus", [P, RING])
        wts = sb("wts", [P, RING])
        diag = sb("diag", [P, SETS, 2, P])
        passed = sb("passed", [P, 1])
        stat = sb("stat", [P, 8])
        half_pi = sb("half_pi", [P, 1])
        mx = sb("mx", [P, NC * HEADS])
        nmx = sb("nmx", [P, NC * HEADS])
        den = sb("den", [P, NC * HEADS])
        rden = sb("rden", [P, NC * HEADS])
        skip = sb("skip", [P, KT])
        ps = ctx.enter_context(nc.psum_tensor("ps", [P, 8, 512], F32))

        ident = con[:, C_ID:C_ID + P]
        ramp = con[:, C_RAMP:C_RAMP + P]
        iota = con[:, C_IOTA:C_IOTA + TOPK]

        def banks(a, b):
            return ps[:, a:b, :].rearrange("p b n -> p (b n)")

        def view(t, at, *shape):
            n = int(np.prod(shape))
            v = t[:, at:at + n]
            if len(shape) == 2:
                v = v.rearrange("p (a b) -> p a b", a=shape[0])
            if len(shape) == 3:
                v = v.rearrange("p (a b c) -> p a b c", a=shape[0], b=shape[1])
            return v

        def spread(ap, axis, shape):
            return ap.unsqueeze(axis).to_broadcast(shape)

        cosT = view(area, 0, PAIRS, P)
        sinT = view(area, 4096, PAIRS, P)
        WB = view(area, 8192, KT, 2, P)
        CW = view(area, 10240, PAIRS, 3, 32)
        M = [[view(area, 13312 + (4 * p + i) * 512, PPT, P) for i in range(4)] for p in range(2)]
        mag, z0re, z0im, zta, ztb = [view(area, 17408 + 32 * i, PAIRS) for i in range(5)]
        sig = view(area, 13312, D)
        craw = view(ringmem, 0, 2, PAIRS, GH)
        tmpc = view(ringmem, 1024, 2, PAIRS, GH)
        small = view(ringmem, 2048, 20, PAIRS)
        wglu = [wt[:, 1]] + [view(ringmem, 4096 * i, KT, BLOCK) for i in (1, 2, 3)]
        (lre, lim, step, xr, turn, whole, frac, sn, cs, lbre, lbim, dn, rdn, ta, tb, cre, cim,
         absf) = [small[:, i, :] for i in (0, 1, 3, 4, 5, 6, 7, 8, 9, 10, 11, 12, 13, 14, 15, 16, 17, 18)]

        gflat = gT[:, :, :].rearrange("p k t -> p (k t)")
        keysT = [view(area, 13312 if ph == 0 else 12800, HP, NKEYS) for ph in range(2 * NC)]
        qT = [view(area, 15360 if ph == 0 else 14848, HP, P) for ph in range(2 * NC)]
        EQ = [view(area, 17600 if ph == 0 else 16896, QSTEPS, TOPK) for ph in range(2 * NC)]
        S2 = view(gflat, 0, QHP, NKEYS)
        cand = view(gflat, 512, QH, TOPK * TOPK)
        qs = sb("qs", [P, 512])
        stop = view(qs, 0, QHP, TOPK)
        itop = view(qs, 64, QHP, TOPK).bitcast(U32)
        itopf = view(qs, 128, QHP, TOPK)
        best, pos, posi, posj, posif, posjf, keyf = [view(qs, 192 + 32 * i, QH, TOPK) for i in range(7)]
        pos, posi, posj = [t.bitcast(U32) for t in (pos, posi, posj)]
        gsum = view(qs, 416, QH)
        grec = view(qs, 418, QH)

        K0 = view(area, 0, NG, 8, P)
        V0 = view(area, 3072, NG, D)
        K1 = view(area, 6144, NG, 4, P)
        V1 = view(area, 7680, NG, BLOCK)
        QT = view(area, 9216, NG, 4, P)
        RA = view(area, 10752, BLOCK)
        RB = view(area, 11264, BLOCK)
        RR = [view(area, 11776 + BLOCK * i, BLOCK) for i in range(2)]
        mask = view(area, 12800, 2 * NG * P)
        SS = [view(area, 13568 + 768 * i, 768) for i in range(2)]
        PT = [view(area, 15104 + 768 * i, 768) for i in range(2)]
        O = view(area, 16640, D)
        ring = view(ringmem, 0, RING, 2 * D)

        x_in = [sem(f"x_in{c}") for c in range(NC)]
        con_in = sem("con_in")
        lam_in = sem("lam_in")
        craw_in = sem("craw_in")
        zeroed = sem("zeroed")
        wb_in = sem("wb_in")
        gain_in = sem("gain_in")
        keys_in = sem("keys_in")
        mask_in = sem("mask_in")
        w_in = [sem(f"w_in{k}") for k in range(2)]
        glu_in = [sem(f"glu_in{i}") for i in range(4)]
        glu_used = sem("glu_used")
        w_used = sem("w_used")
        dve = sem("dve_step")
        act_step = sem("act_step")
        var_ready = sem("var_ready")
        root_ready = sem("root_ready")
        normed = sem("normed")
        turned = sem("turned")
        hT_ready = sem("hT_ready")
        lam_dve = sem("lam_dve")
        lam_act = sem("lam_act")
        tab_dve = sem("tab_dve")
        tab_act = sem("tab_act")
        cw_ready = sem("cw_ready")
        bu_ready = sem("bu_ready")
        bu_used = sem("bu_used")
        prod_ready = sem("prod_ready")
        y_ready = sem("y_ready")
        y_skip = sem("y_skip")
        y_gelu = sem("y_gelu")
        sig_ready = sem("sig_ready")
        glu_done = sem("glu_done")
        q_copied = sem("q_copied")
        score_done = sem("score_done")
        score_copied = sem("score_copied")
        best_ready = sem("best_ready")
        gate_exp = sem("gate_exp")
        idx_ready = sem("idx_ready")
        rows_ready = sem("rows_ready")
        landed = [sem(f"landed{i}") for i in range(RING)]
        dots_ready = sem("dots_ready")
        gelu_ready = sem("gelu_ready")
        wts_ready = sem("wts_ready")
        diag_ready = sem("diag_ready")
        v_pe = sem("v_pe")
        v_dve = sem("v_dve")
        peer_done = sem("peer_done")
        acc_evac = sem("acc_evac")
        roped = sem("roped")
        qk_turned = sem("qk_turned")
        qk_copied = sem("qk_copied")
        s_done = sem("s_done")
        s_masked = sem("s_masked")
        nmx_ready = sem("nmx_ready")
        p_ready = sem("p_ready")
        p_turned = sem("p_turned")
        pT_copied = sem("pT_copied")
        pv_done = sem("pv_done")
        o_scaled = sem("o_scaled")
        o_turned = sem("o_turned")
        oT_ready = sem("oT_ready")
        wo_done = sem("wo_done")
        out_ready = sem("out_ready")
        out_done = sem("out_done")

        block = ctx.enter_context(nc.Block())

        class Gather:

            def __init__(self, eng, pair):
                self.eng, self.pair, self.done = eng, pair, 0

            def at(self, phase, n):
                if phase is None:
                    return
                for end in SEGMENTS[1:]:
                    self.upto(phase, PAIRS_G * phase + min(n, end))

            def upto(self, phase, upto):
                while self.done < upto:
                    b, r = divmod(self.done, SETS)
                    p = self.done % PAIRS_G
                    last = (upto // SETS if upto % PAIRS_G else upto // SETS - 1)
                    if r == 0 and p and last - b >= 2:
                        with self.eng.Fori(b, last) as i:
                            for r in range(SETS):
                                self.pair(r, i, phase, i - phase * ROUNDS, False, False,
                                          both_on_pe(phase, p + r))
                        self.done = last * SETS
                        continue
                    self.pair(r, b, phase, b - phase * ROUNDS, p == 0, p == PAIRS_G - 1,
                              both_on_pe(phase, p))
                    self.done += 1

        TOPK_PARTS = 4
        S5_AT, S5_K = 14, 4
        GLU_AT, NORM1_AT, WQ_AT = 46, 51, 54
        QKV_AT = 6
        HEADS_AT = (17, 17)
        HEAD_TICKS = (2, 1)
        HALF_AT = (17, 21)
        WO_AT = (40, 49)


        @block.sync
        def _(sp):
            sp.dma_start(X[:, 0, :], x[0:P, :]).then_inc(x_in[0], 16)
            sp.dma_start(small[:, 0:3, :], lam).then_inc(lam_in, 16)
            sp.dma_start(con[:, :], consts).then_inc(con_in, 16)
            sp.dma_start(skip[:, :], d_skip).then_inc(lam_in, 16)
            sp.dma_start(gain[:, :], gains[0:1, :].to_broadcast([P, D])).then_inc(gain_in, 16)
            sp.dma_start(craw[:, :, :, :], c_out).then_inc(craw_in, 16)
            sp.wait_ge(zeroed, 1)
            for g in range(KT):
                for r in range(2):
                    a = g % 2
                    sp.dma_start(WB[GH * g:GH * (g + 1), :, r, a * STATE:(a + 1) * STATE],
                                 b_in[r, g]).then_inc(wb_in, 16)
            sp.dma_start(X[:, 1, :], x[P:2 * P, :]).then_inc(x_in[1], 16)

            def weights(layer, c, first, last):
                for i in range(first, last):
                    n = item(layer, c, i)
                    if layer == 0:
                        src = (w_glu[:, i * BLOCK:(i + 1) * BLOCK] if i < WQ0 else
                               w_q[0, :, (i - WQ0) * BLOCK:(i - WQ0 + 1) * BLOCK])
                    elif i < WO:
                        half, j = divmod(i, 9)
                        src = w_qkv[:, j * D + half * BLOCK:j * D + (half + 1) * BLOCK]
                    elif i < WQ1:
                        src = w_o[:, (i - WO) * BLOCK:(i - WO + 1) * BLOCK]
                    else:
                        src = w_q[1, :, (i - WQ1) * BLOCK:(i - WQ1 + 1) * BLOCK]
                    if n == 1:
                        sp.wait_ge(glu_used, 1)
                    if n >= 2:
                        sp.wait_ge(w_used, n - 1)
                    sp.dma_start(wt[:, n % 2], src.rearrange("(k p) n -> p k n", p=P)).then_inc(w_in[n % 2], 16)

            def next_gain(e, n):
                sp.wait_ge(normed, e)
                sp.dma_start(gain[:, :], gains[n:n + 1, :].to_broadcast([P, D])).then_inc(gain_in, 16)

            def load_keys(phase, ready, count):
                sp.wait_ge(ready, count)
                sp.dma_start(keysT[phase], keys[phase // NC]).then_inc(keys_in, 16)

            for i in range(4):
                sp.dma_start(wglu[i], w_glu[:, i * BLOCK:(i + 1) * BLOCK].rearrange(
                    "(k p) n -> p k n", p=P)).then_inc(glu_in[i], 16)
            weights(0, 0, 4, 5)
            next_gain(1, 1)
            weights(0, 0, 5, 6)
            load_keys(0, glu_done, 1)
            weights(0, 0, 6, 8)
            next_gain(2, 0)
            weights(0, 1, 0, 2)
            next_gain(3, 1)
            weights(0, 1, 2, 6)
            load_keys(1, glu_done, 2)
            weights(0, 1, 6, 8)
            for c in range(NC):
                next_gain(4 + 2 * c, 2)
                weights(1, c, 0, 2)
                next_gain(5 + 2 * c, 3)
                weights(1, c, 2, 8)
                sp.wait_ge(idx_ready, QUARTERS * (2 + c))
                n = NG * P * (c + 1)
                sp.dma_start(mask[:, 0:n], masks[:, M_AT[c]:M_AT[c] + n]).then_inc(mask_in, 16)
                weights(1, c, 8, WO + 1)
                load_keys(2 + c, o_turned, c + 1)
                weights(1, c, WO + 1, ITEMS1)
            next_gain(8, 4)
            for c in range(NC):
                sp.wait_ge(out_ready, c + 1)
                sp.dma_start(out[c * P:(c + 1) * P, :], H[:, c, :]).then_inc(out_done, 16)
            sp.wait_ge(out_done, 16 * NC)

        @block.tensor
        def _(pe):
            def pair(r, b, phase, _, first, final, both):
                pe.wait_ge(diag_ready, b * SETS + (r + 1))
                if first and phase:
                    pe.wait_ge(peer_done, phase)
                for i in range(2 if both else 1):
                    for n in range(2):
                        last = pe.matmul(ps[:, n, :], diag[:, r, i, :],
                                         ring[:, 2 * r + i, D + n * 512:D + (n + 1) * 512],
                                         start=(first and i == 0), stop=final, skip_group_check=True)
                last.then_inc(v_pe, 1)

            g = Gather(pe, pair)

            def turn(src, event):
                pe.wait_ge(normed, event + 1)
                for k in range(KT):
                    last = pe.transpose(ps[:, 2 + k // 4, (k % 4) * P:(k % 4 + 1) * P],
                                        src[:, k * P:(k + 1) * P], ident)
                last.then_inc(turned, 1)

            def project(n, bank, act):
                pe.wait_ge(w_in[n % 2], 16 * (n // 2 + 1))
                for k in range(KT):
                    last = pe.matmul(ps[:, bank, :], act[:, k, :], wt[:, n % 2, k, :], start=(k == 0),
                                     stop=(k == KT - 1))
                last.then_inc(w_used, 1)

            def project_turned(n, bank):
                pe.wait_ge(w_in[n % 2], 16 * (n // 2 + 1))
                for k in range(KT):
                    for m in range(4):
                        last = pe.matmul(ps[:, bank, m * P:(m + 1) * P], wt[:, n % 2, k, m * P:(m + 1) * P],
                                         hT[:, k, :], start=(k == 0 and m == 0), stop=(k == KT - 1),
                                         skip_group_check=True)
                last.then_inc(w_used, 1)

            def peer_scores(gphase, layer, c, at_norm, at_wq):
                e, ph = norm_event(layer, c, 1), NC * layer + c
                g.at(gphase, at_norm + 2)
                turn(H[:, c, :], e)
                for i in range(QUARTERS + 1):
                    g.at(gphase, at_wq + i)
                    if i == 0:
                        pe.wait_ge(hT_ready, e + 1)
                    if i < QUARTERS:
                        project_turned(item(layer, c, (WQ0, WQ1)[layer] + i), 4 + i)
                    if i == 1:
                        pe.wait_ge(keys_in, 16 * (ph + 1))
                    if i >= 1:
                        pe.wait_ge(q_copied, QUARTERS * ph + i)
                        for m in range(QHP):
                            hp = QHP * (i - 1) + m
                            last = pe.matmul(ps[:, 3 + i, m * P:(m + 1) * P], qT[ph][:, hp, :],
                                             keysT[ph][:, hp, :], start=True, stop=True,
                                             skip_group_check=True)
                        last.then_inc(score_done, 1)

            def s5_bu(c, k):
                u = KT * c + k
                if k >= 1:
                    pe.wait_ge(bu_used, u)
                for q in range(PPT):
                    rows = slice(32 * q, 32 * (q + 1))
                    for r in range(2):
                        last = pe.matmul(ps[:, 4 + q, r * P:(r + 1) * P], WB[rows, k, r, :],
                                         hT[rows, k, :], start=True, stop=True, skip_group_check=True)
                last.then_inc(bu_ready, 1)

            def s5_y(c, k):
                u = KT * c + k
                pe.wait_ge(prod_ready, u + 1)
                if k == 0 and c == 0:
                    pe.wait_ge(cw_ready, 6)
                if k >= 1:
                    pe.wait_ge(y_skip, u)
                m1, m2, m3, m4 = M[k % 2]
                for q in range(PPT):
                    for i, (w, m) in enumerate(((0, m1), (1, m3), (2, m2), (2, m4))):
                        last = pe.matmul(ps[32 * q:32 * (q + 1), 2, 0:P],
                                         CW[:, PPT * k + q, w, :], m[:, q, :], start=(i == 0),
                                         stop=(i == 3))
                last.then_inc(y_ready, 1)

            def glu_first(k):
                pe.wait_ge(y_gelu, k + 1)
                for i, bank in ((2, 0), (3, 1), (0, 3)):
                    if k == 0:
                        pe.wait_ge(glu_in[i], 16)
                    last = pe.matmul(ps[:, bank, :], gT[:, k, :], wglu[i][:, k, :], start=(k == 0),
                                     stop=(k == KT - 1))
                if k == KT - 1:
                    last.then_inc(glu_used, 1)
                    pe.wait_ge(glu_in[1], 16)
                    for n in range(KT):
                        last = pe.matmul(ps[:, 4, :], gT[:, n, :], wglu[1][:, n, :], start=(n == 0),
                                         stop=(n == KT - 1))
                    last.then_inc(glu_used, 1)

            def layer0(gphase, c):
                e = norm_event(0, c, 0)
                turn(H[:, c, :], e)
                g.at(gphase, S5_AT)
                pe.wait_ge(hT_ready, e + 1)
                if c == 0:
                    pe.wait_ge(wb_in, 16 * 2 * KT)
                else:
                    pe.wait_ge(idx_ready, QUARTERS)
                s5_bu(c, 0)
                for k in range(KT):
                    g.at(gphase, S5_AT + S5_K * (k + 1) - 1)
                    if k + 1 < KT:
                        s5_bu(c, k + 1)
                    s5_y(c, k)
                    if c == 0 and k:
                        glu_first(k - 1)
                if c == 0:
                    glu_first(KT - 1)
                for i in range(4 * c):
                    g.at(gphase, GLU_AT + i)
                    if i == 0:
                        pe.wait_ge(y_gelu, KT * (c + 1))
                    project(item(0, c, GLU + i), 4 + i, gT)
                peer_scores(gphase, 0, c, NORM1_AT, WQ_AT)

            def attn_turn(n):
                m = 2 * (n // 3) + n % 3
                pe.wait_ge(roped, m + 1)
                if m >= 2:
                    pe.wait_ge(qk_copied, m - 1)
                for j in range(4):
                    last = pe.transpose(ps[:, 4 + m % 2, j * P:(j + 1) * P],
                                        RR[m % 2][:, j * P:(j + 1) * P], ident)
                last.then_inc(qk_turned, 1)

            def attn_s(c, half, h):
                u = HEADS * c + NH * half + h
                rows = slice(DH * (h % 2), DH * (h % 2 + 1))
                if h >= 2 - c:
                    pe.wait_ge(s_masked, u - 1 + c)
                for gr in range(NG):
                    for kb in range(c + 1):
                        at = (1 - c) * 512 * (u % 2) + (gr * (c + 1) + kb) * P
                        kt = K0[rows, gr, 4 * half + h // 2, :] if kb == 0 else K1[rows, gr, h // 2, :]
                        last = pe.matmul(ps[:, 2 + at // 512, at % 512:at % 512 + P],
                                         QT[rows, gr, h // 2, :], kt, start=True, stop=True,
                                         skip_group_check=True)
                last.then_inc(s_done, 1)

            def attn_pt(c, half, h):
                u = HEADS * c + NH * half + h
                pe.wait_ge(p_ready, u + 1)
                if u:
                    pe.wait_ge(pT_copied, u)
                for j in range(NG * (c + 1)):
                    last = pe.transpose(ps[:, 5 + j // 4, (j % 4) * P:(j % 4 + 1) * P],
                                        SS[u % 2][:, j * P:(j + 1) * P], ident)
                last.then_inc(p_turned, 1)

            def attn_pv(c, half, h):
                u = HEADS * c + NH * half + h
                pe.wait_ge(pT_copied, u + 1)
                if h == 0 and u:
                    pe.wait_ge(o_scaled, 2 * c + half)
                n = NG * (c + 1)
                for j in range(n):
                    gr, kb = divmod(j, c + 1)
                    vv = (V0[:, gr, (NH * half + h) * DH:(NH * half + h + 1) * DH] if kb == 0 else
                          V1[:, gr, h * DH:(h + 1) * DH])
                    last = pe.matmul(ps[:, 7, h * DH:(h + 1) * DH], PT[u % 2][:, j * P:(j + 1) * P], vv,
                                     start=(j == 0), stop=(j == n - 1), skip_group_check=True)
                last.then_inc(pv_done, 1)

            def layer1(gphase, c):
                e = norm_event(1, c, 0)
                g.at(gphase, 3)
                turn(H[:, c, :], e)
                for half in range(2):
                    base = QKV_AT + HALF_AT[c] * half
                    for j in range(11):
                        g.at(gphase, base + j)
                        n = 9 * (2 * c + half) + j
                        if j < 9:
                            if j == 0 and half == 0:
                                pe.wait_ge(hT_ready, e + 1)
                            if j == 0 and half == 1:
                                pe.wait_ge(s_masked, HEADS * c + NH)
                            if j >= 2:
                                pe.wait_ge(acc_evac, n - 1)
                            project(item(1, c, QKV + 9 * half + j), 2 + j % 2, hT)
                        if j == 2 and half == 0:
                            pe.wait_ge(idx_ready, QUARTERS * (c + 1) + 2)
                        if j >= 2 and (j - 2) % 3 < 2:
                            attn_turn(n - 2)
                    base = HEADS_AT[c] + HALF_AT[c] * half
                    for i in range(NH + 3):
                        g.at(gphase, base + i // HEAD_TICKS[c])
                        if i == 0:
                            pe.wait_ge(idx_ready, QUARTERS * (c + 2))
                            pe.wait_ge(qk_copied, 6 * (2 * c + half + 1))
                            pe.wait_ge(acc_evac, 9 * (2 * c + half + 1))
                        if 2 <= i < NH + 2:
                            attn_pt(c, half, i - 2)
                        if i >= 3:
                            attn_pv(c, half, i - 3)
                        if i < NH:
                            attn_s(c, half, i)
                g.at(gphase, WO_AT[c])
                pe.wait_ge(o_scaled, 2 * (c + 1))
                for k in range(KT):
                    last = pe.transpose(ps[:, 2 + k // 4, (k % 4) * P:(k % 4 + 1) * P],
                                        O[:, k * P:(k + 1) * P], ident)
                last.then_inc(o_turned, 1)
                for i in range(2):
                    g.at(gphase, WO_AT[c] + 1 + i)
                    if i == 0:
                        pe.wait_ge(oT_ready, c + 1)
                    project(item(1, c, WO + i), 4 + i, gT)
                peer_scores(gphase, 1, c, WO_AT[c] + 3, WO_AT[c] + 7)

            pe.wait_ge(con_in, 16)
            layer0(None, 0)
            layer0(0, 1)
            g.at(0, PAIRS_G)
            layer1(1, 0)
            g.at(1, PAIRS_G)
            layer1(2, 1)
            g.at(2, PAIRS_G)
            g.at(3, PAIRS_G)

        @block.scalar
        def _(act):
            steps = [0]

            def link(ins):
                steps[0] += 1
                ins.then_inc(act_step, 1)
                act.wait_ge(act_step, steps[0])

            def pair(r, b, phase, _, first, final, both):
                act.wait_ge(dots_ready, b * SETS + (r + 1))
                act.activation(gelus[:, 2 * r:2 * r + 2], dots[:, 2 * r:2 * r + 2],
                               ACT.Gelu_apprx_tanh).then_inc(gelu_ready, 1)
                act.wait_ge(wts_ready, b * SETS + (r + 1))
                for i in range(2 if both else 1):
                    last = act.activation(diag[:, r, i, :], ident, ACT.Copy,
                                          scale=wts[:, 2 * r + i:2 * r + i + 1])
                last.then_inc(diag_ready, 1)

            g = Gather(act, pair)

            def root(e):
                act.wait_ge(var_ready, e + 1)
                act.activation(stat[:, 2:3], stat[:, 1:2], ACT.Sqrt).then_inc(root_ready, 1)

            def copy_turn(dst, src_ready, count, done):
                act.wait_ge(src_ready, count)
                act.copy(dst[:, :, :].rearrange("p k t -> p (k t)"), banks(2, 4)).then_inc(done, 1)

            def peer_scores(gphase, layer, c, at_norm, at_wq):
                e, ph = norm_event(layer, c, 1), NC * layer + c
                g.at(gphase, at_norm + 1)
                root(e)
                g.at(gphase, at_norm + 3)
                copy_turn(hT, turned, e + 1, hT_ready)
                for i in range(QUARTERS):
                    g.at(gphase, at_wq + 1 + i)
                    act.wait_ge(w_used, item(layer, c, (WQ0, WQ1)[layer] + i) + 1)
                    act.copy(qT[ph][:, QHP * i:QHP * (i + 1), :].rearrange("p k t -> p (k t)"),
                             ps[:, 4 + i, :]).then_inc(q_copied, 1)
                g.at(gphase, at_wq + 1 + TOPK_PARTS)
                gate_quarter(ph, 0)

            def gate_quarter(ph, i):
                act.wait_ge(best_ready, QUARTERS * ph + i + 1)
                gq = gate[:, ph % NC, QSTEPS * i:QSTEPS * (i + 1)]
                act.activation(gq, gq, ACT.Exp).then_inc(gate_exp, 1)

            def other_gates(ph, apart):
                for i in range(1, QUARTERS):
                    g.at(ph, apart * (TOPK_PARTS * i - 1) + 1)
                    gate_quarter(ph, i)

            def layer0(gphase, c):
                e = norm_event(0, c, 0)
                root(e)
                copy_turn(hT, turned, e + 1, hT_ready)
                if c == 1:
                    other_gates(0, 1)
                if c == 0:
                    for k in range(KT):
                        q = slice(PPT * k, PPT * (k + 1))
                        act.wait_ge(tab_dve, k + 1)
                        link(act.activation(cosT[:, q, :], sinT[:, q, :], ACT.Abs))
                        act.activation(cosT[:, q, :], cosT[:, q, :], ACT.Sin, bias=half_pi[:, 0:1], scale=-TWO_PI)
                        act.activation(sinT[:, q, :], sinT[:, q, :], ACT.Sin, scale=TWO_PI).then_inc(tab_act, 1)
                for k in range(KT):
                    g.at(gphase, S5_AT + S5_K * (k + 1))
                    act.wait_ge(y_skip, KT * c + k + 1)
                    act.activation(gT[:, k, :], gT[:, k, :], ACT.Gelu_apprx_tanh).then_inc(y_gelu, 1)
                g.at(gphase, GLU_AT + 4)
                if c == 0:
                    act.wait_ge(glu_used, 1)
                else:
                    act.wait_ge(w_used, item(0, c, GLU + 4))
                act.activation(sig, banks(0, 2) if c == 0 else banks(6, 8), ACT.Sigmoid).then_inc(sig_ready, 1)
                peer_scores(gphase, 0, c, NORM1_AT, WQ_AT)

            def exp_p(c, half, h):
                u, n = HEADS * c + NH * half + h, NG * P * (c + 1)
                act.wait_ge(nmx_ready, u + 1)
                act.activation(SS[u % 2][:, 0:n], SS[u % 2][:, 0:n], ACT.Exp, bias=nmx[:, u:u + 1],
                               scale=DH ** -0.5, accum_out=den[:, u:u + 1]).then_inc(p_ready, 1)

            def copy_pt(c, half, h):
                u, n = HEADS * c + NH * half + h, NG * P * (c + 1)
                act.wait_ge(p_turned, u + 1)
                if u >= 2:
                    act.wait_ge(pv_done, u - 1)
                act.copy(PT[u % 2][:, 0:n], banks(5, 7)[:, 0:n]).then_inc(pT_copied, 1)

            def layer1(gphase, c):
                e = norm_event(1, c, 0)
                g.at(gphase, 1)
                root(e)
                g.at(gphase, 4)
                copy_turn(hT, turned, e + 1, hT_ready)
                gate_quarter(c + 1, 1)
                for half in range(2):
                    base = QKV_AT + HALF_AT[c] * half
                    for j in range(9 + 3):
                        g.at(gphase, base + j)
                        if half == 0 and j in (2, 6):
                            gate_quarter(c + 1, 2 if j == 2 else 3)
                        if j >= 1 and j <= 9 and (j - 1) % 3 == 2:
                            act.wait_ge(w_used, item(1, c, QKV + 9 * half + j))
                            gr = (j - 1) // 3
                            dst = V0[:, gr, half * BLOCK:(half + 1) * BLOCK] if c == 0 else V1[:, gr, :]
                            act.copy(dst, ps[:, 2 + (j - 1) % 2, :]).then_inc(acc_evac, 1)
                        if j >= 3 and (j - 3) % 3 < 2:
                            gr, k = divmod(j - 3, 3)
                            m = 6 * (2 * c + half) + 2 * gr + k
                            act.wait_ge(qk_turned, m + 1)
                            dst = (QT[:, gr] if k == 0 else
                                   K0[:, gr, 4 * half:4 * half + 4, :] if c == 0 else K1[:, gr])
                            act.copy(dst.rearrange("p m t -> p (m t)"), ps[:, 4 + m % 2, :]).then_inc(qk_copied, 1)
                    base = HEADS_AT[c] + HALF_AT[c] * half
                    for i in range(1, NH + 3):
                        g.at(gphase, base + i // HEAD_TICKS[c])
                        if i - 1 < NH:
                            exp_p(c, half, i - 1)
                        if i >= 3:
                            copy_pt(c, half, i - 3)
                g.at(gphase, WO_AT[c] + 1)
                copy_turn(gT, o_turned, c + 1, oT_ready)
                peer_scores(gphase, 1, c, WO_AT[c] + 3, WO_AT[c] + 7)

            act.wait_ge(lam_in, 32)
            act.activation(step, small[:, 2, :], ACT.Exp).then_inc(lam_act, 1)
            act.wait_ge(lam_dve, 1)
            act.activation(mag, xr, ACT.Exp).then_inc(lam_act, 1)
            act.wait_ge(lam_dve, 2)
            act.activation(sn, frac, ACT.Sin, scale=TWO_PI).then_inc(lam_act, 1)
            act.wait_ge(zeroed, 3)
            link(act.activation(absf, frac, ACT.Abs))
            act.activation(cs, absf, ACT.Sin, bias=half_pi[:, 0:1], scale=-TWO_PI).then_inc(lam_act, 1)
            layer0(None, 0)
            layer0(0, 1)
            g.at(0, PAIRS_G)
            layer1(1, 0)
            g.at(1, PAIRS_G)
            layer1(2, 1)
            g.at(2, PAIRS_G)
            other_gates(3, 3)
            g.at(3, 3 * 3 * TOPK_PARTS + 4)
            root(8)
            g.at(3, PAIRS_G)
            root(9)

        @block.gpsimd
        def _(pool):
            pool.memset(WB.rearrange("p a b c -> p (a b c)"), 0.0).then_inc(zeroed, 1)
            pool.memset(CW.rearrange("p a b c -> p (a b c)"), 0.0).then_inc(zeroed, 1)
            pool.memset(half_pi[:, :], HALF_PI).then_inc(zeroed, 1)

            def pair(phase, b, r, first):
                c = phase % NC
                if not first:
                    pool.wait_ge(v_pe, b * SETS + (phase * PAIRS_G + r - SETS + 1))
                    pool.wait_ge(v_dve, b * SETS + (phase * PAIRS_G + r - SETS + 1))
                at = bass.ds(b * RING + 2 * r, 2)
                pool.tensor_tensor(rows_now[:, r, :], row_a[:, c, at], row_b[:, c, at],
                                   ALU.add).then_inc(rows_ready, 1)
                pool.wait_ge(rows_ready, b * SETS + (phase * PAIRS_G + r + 1))
                pool.tensor_tensor(tick[:, :], rows_now[:, r, 0:1], rows_now[:, r, 0:1], ALU.add)
                for i in range(2):
                    pool.indirect_dma_start(
                        ring[:, 2 * r + i, :], None, experts[phase // NC],
                        bass.IndirectOffsetOnAxis(ap=rows_now[:, r, i:i + 1], axis=0)
                    ).then_inc(landed[2 * r + i], 16)

            for phase in range(2 * NC):
                for i in range(QUARTERS):
                    pool.wait_ge(idx_ready, QUARTERS * phase + i + 1)
                    start = i * ROUNDS // QUARTERS
                    if phase == 0 and i == 0:
                        for r in range(SETS):
                            pair(0, 0, r, first=True)
                        start = 1
                    with pool.Fori(start, (i + 1) * ROUNDS // QUARTERS) as b:
                        for r in range(SETS):
                            pair(phase, b, r, first=False)

        @block.vector
        def _(v):
            steps = [0]

            def link(ins):
                steps[0] += 1
                ins.then_inc(dve, 1)
                v.wait_ge(dve, steps[0])

            def pair(r, b, phase, bp, first, final, both):
                c = phase % NC
                for i in (2 * r, 2 * r + 1):
                    v.wait_ge(landed[i], b * 16 + 16)
                    last = v.tensor_tensor_reduce(ring[:, i, 0:D], ring[:, i, 0:D], H[:, c, :],
                                                  1.0, 0.0, ALU.mult, ALU.add, dots[:, i:i + 1])
                last.then_inc(dots_ready, 1)
                v.wait_ge(gelu_ready, b * SETS + (r + 1))
                v.tensor_tensor(wts[:, 2 * r:2 * r + 2], gelus[:, 2 * r:2 * r + 2],
                                gate[:, c, bass.ds(bp * RING + 2 * r, 2)], ALU.mult).then_inc(wts_ready, 1)
                v.wait_ge(wts_ready, b * SETS + (r + 1))
                if both:
                    v.tensor_copy(passed[:, :], wts[:, 2 * r:2 * r + 1]).then_inc(v_dve, 1)
                    return
                if not (first and phase == 0):
                    v.wait_ge(v_dve, b * SETS + r)
                v.scalar_tensor_tensor(out=X[:, c, :], in0=ring[:, 2 * r + 1, D:2 * D],
                                       scalar=wts[:, 2 * r + 1:2 * r + 2], in1=X[:, c, :],
                                       op0=ALU.mult, op1=ALU.add).then_inc(v_dve, 1)

            g = Gather(v, pair)

            def peer_end(phase):
                c = phase % NC
                g.at(phase, PAIRS_G)
                v.wait_ge(v_pe, PAIRS_G * (phase + 1))
                v.wait_ge(v_dve, PAIRS_G * (phase + 1))
                v.tensor_tensor(X[:, c, :], X[:, c, :], banks(0, 2), ALU.add).then_inc(peer_done, 1)

            def norm(gphase, start, c, e, done, count):
                link(v.tensor_tensor_reduce(H[:, c, :], X[:, c, :], X[:, c, :], 1.0, 0.0, ALU.mult,
                                            ALU.add, stat[:, 0:1]))
                v.tensor_scalar(stat[:, 1:2], stat[:, 0:1], 1.0 / D, EPS, ALU.mult,
                                ALU.add).then_inc(var_ready, 1)
                g.at(gphase, start + 1)
                v.wait_ge(root_ready, e + 1)
                link(v.reciprocal(stat[:, 3:4], stat[:, 2:3]))
                v.wait_ge(gain_in, 16 * (min(e, 8) + 1))
                v.scalar_tensor_tensor(out=H[:, c, :], in0=X[:, c, :], scalar=stat[:, 3:4],
                                       in1=gain[:, :], op0=ALU.mult, op1=ALU.mult).then_inc(done, 1)

            def s5_lambda():
                v.wait_ge(lam_in, 32)
                v.wait_ge(lam_act, 1)
                v.tensor_tensor(xr, lre, step, ALU.mult).then_inc(lam_dve, 1)
                link(v.tensor_tensor(turn, lim, step, ALU.mult))
                link(v.tensor_scalar(turn, turn, 1.0 / (2.0 * np.pi), None, ALU.mult))
                link(v.tensor_scalar(whole, turn, ROUND, -ROUND, ALU.add, ALU.add))
                v.tensor_tensor(frac, turn, whole, ALU.subtract).then_inc(lam_dve, 1)
                v.wait_ge(lam_dve, 2)

            def s5_tables():
                v.wait_ge(con_in, 16)
                for k in range(KT):
                    q = slice(PPT * k, PPT * (k + 1))
                    shape = [P, PPT, P]
                    link(v.tensor_tensor(sinT[:, q, :], spread(ramp, 1, shape),
                                         spread(frac[:, q], 2, shape), ALU.mult))
                    link(v.tensor_scalar(cosT[:, q, :], sinT[:, q, :], ROUND, -ROUND, ALU.add, ALU.add))
                    v.tensor_tensor(sinT[:, q, :], sinT[:, q, :], cosT[:, q, :],
                                    ALU.subtract).then_inc(tab_dve, 1)

            def s5_coef():
                v.wait_ge(lam_act, 4)
                v.tensor_tensor(lbim, mag, sn, ALU.mult)
                v.tensor_tensor(ta, lre, lre, ALU.mult)
                v.tensor_tensor(tb, lim, lim, ALU.mult)
                link(v.tensor_tensor(lbre, mag, cs, ALU.mult))
                v.tensor_tensor(dn, ta, tb, ALU.add)
                link(v.tensor_scalar(lbre, lbre, -1.0, None, ALU.add))
                v.reciprocal(rdn, dn)
                v.tensor_tensor(ta, lbre, lre, ALU.mult)
                link(v.tensor_tensor(tb, lbim, lim, ALU.mult))
                link(v.tensor_tensor(cre, ta, tb, ALU.add))
                v.tensor_tensor(cre, cre, rdn, ALU.mult)
                v.tensor_tensor(ta, lbim, lre, ALU.mult)
                link(v.tensor_tensor(tb, lbre, lim, ALU.mult))
                link(v.tensor_tensor(cim, ta, tb, ALU.subtract))
                link(v.tensor_tensor(cim, cim, rdn, ALU.mult))
                v.wait_ge(craw_in, 16)
                v.wait_ge(zeroed, 3)
                shape = [P, PAIRS, GH]
                re, im = spread(cre, 2, shape), spread(cim, 2, shape)
                v.tensor_tensor(tmpc[:, 0], craw[:, 0], re, ALU.mult)
                link(v.tensor_tensor(tmpc[:, 1], craw[:, 1], im, ALU.mult))
                link(v.tensor_tensor(tmpc[:, 0], tmpc[:, 0], tmpc[:, 1], ALU.subtract))
                for a in range(2):
                    half = slice(STATE * a, STATE * (a + 1))
                    cols = slice(GH * a, GH * (a + 1))
                    v.tensor_copy(CW[half, :, 0, cols], tmpc[half, 0]).then_inc(cw_ready, 1)
                    v.tensor_scalar(CW[half, :, 1, cols], tmpc[half, 0], -1.0, None,
                                    ALU.mult).then_inc(cw_ready, 1)
                v.wait_ge(cw_ready, 4)
                v.tensor_tensor(tmpc[:, 0], craw[:, 0], im, ALU.mult)
                link(v.tensor_tensor(tmpc[:, 1], craw[:, 1], re, ALU.mult))
                link(v.tensor_tensor(tmpc[:, 0], tmpc[:, 0], tmpc[:, 1], ALU.add))
                for a in range(2):
                    half = slice(STATE * a, STATE * (a + 1))
                    cols = slice(GH * a, GH * (a + 1))
                    v.tensor_scalar(CW[half, :, 2, cols], tmpc[half, 0], -1.0, None,
                                    ALU.mult).then_inc(cw_ready, 1)

            def tile_of(t, k):
                return t[:, PPT * k:PPT * (k + 1), :]

            def s5_rotate(c, k):
                m1, m2, m3, m4 = M[k % 2]
                u = KT * c + k
                v.wait_ge(bu_ready, u + 1)
                v.wait_ge(tab_act, k + 1)
                if u >= 2:
                    v.wait_ge(y_ready, u - 1)
                co, si = tile_of(cosT, k), tile_of(sinT, k)
                bre, bim = ps[:, 4:8, 0:P], ps[:, 4:8, P:2 * P]
                v.tensor_tensor(m1, co, bre, ALU.mult)
                v.tensor_tensor(m2, si, bim, ALU.mult)
                v.tensor_tensor(m3, co, bim, ALU.mult)
                v.tensor_tensor(m4, si, bre, ALU.mult).then_inc(bu_used, 1)
                v.wait_ge(bu_used, u + 1)
                v.tensor_tensor(m1, m1, m2, ALU.add)
                link(v.tensor_tensor(m3, m3, m4, ALU.subtract))

            def s5_scan(c, k):
                m1, m2, m3, m4 = M[k % 2]
                u = KT * c + k
                for src, dst, z0 in ((m1, m2, z0re), (m3, m4, z0im)):
                    for q in range(PPT):
                        n = PPT * k + q
                        last = v.tensor_tensor_scan(dst[:, q, :], mag[:, n:n + 1].to_broadcast([P, P]),
                                                    src[:, q, :], z0[:, n:n + 1] if c else 0.0,
                                                    ALU.mult, ALU.add)
                link(last)
                co, si, q = tile_of(cosT, k), tile_of(sinT, k), slice(PPT * k, PPT * (k + 1))
                if c == 0:
                    end = slice(P - 1, P)
                    def col(t):
                        return t[:, q].unsqueeze(2)
                    v.tensor_tensor(col(z0re), co[:, :, end], m2[:, :, end], ALU.mult)
                    v.tensor_tensor(col(zta), si[:, :, end], m4[:, :, end], ALU.mult)
                    v.tensor_tensor(col(z0im), si[:, :, end], m2[:, :, end], ALU.mult)
                    link(v.tensor_tensor(col(ztb), co[:, :, end], m4[:, :, end], ALU.mult))
                    v.tensor_tensor(z0re[:, q], z0re[:, q], zta[:, q], ALU.subtract)
                    link(v.tensor_tensor(z0im[:, q], z0im[:, q], ztb[:, q], ALU.add))
                v.tensor_tensor(m1, co, m2, ALU.mult)
                v.tensor_tensor(m3, si, m4, ALU.mult)
                v.tensor_tensor(m2, si, m2, ALU.mult)
                v.tensor_tensor(m4, co, m4, ALU.mult).then_inc(prod_ready, 1)

            def s5_skip(c, k):
                v.wait_ge(y_ready, KT * c + k + 1)
                v.scalar_tensor_tensor(out=gT[:, k, :], in0=hT[:, k, :], scalar=skip[:, k:k + 1],
                                       in1=ps[:, 2, 0:P], op0=ALU.mult,
                                       op1=ALU.add).then_inc(y_skip, 1)

            def layer0(gphase, c):
                if c == 0:
                    s5_tables()
                    s5_coef()
                for k in range(KT):
                    if k == 0:
                        g.at(gphase, S5_AT + 1)
                        s5_rotate(c, 0)
                    g.at(gphase, S5_AT + S5_K * k + 1)
                    s5_scan(c, k)
                    g.at(gphase, S5_AT + S5_K * (k + 1))
                    if k + 1 < KT:
                        s5_rotate(c, k + 1)
                    s5_skip(c, k)
                g.at(gphase, GLU_AT + 5)
                v.wait_ge(sig_ready, c + 1)
                if c == 0:
                    v.wait_ge(glu_used, 2)
                link(v.tensor_tensor(sig, sig, banks(3, 5) if c == 0 else banks(4, 6), ALU.mult))
                v.tensor_tensor(X[:, c, :], X[:, c, :], sig, ALU.add).then_inc(glu_done, 1)
                v.wait_ge(glu_done, c + 1)
                norm(gphase, NORM1_AT, c, norm_event(0, c, 1), normed, 0)
                top_k(gphase, WQ_AT + 2, c, 0)

            def top_k(gphase, start, ph, i):
                for part in range(TOPK_PARTS):
                    g.at(gphase, start + part)
                    top_k_part(ph, i, part)

            def top_k_part(ph, i, part):
                c = ph % NC
                (best_of_halves, sum_pairs, best_of_sums, find_experts)[part](ph, c, i)

            def best_of_halves(ph, c, i):
                S = ps[:, 4 + i, :].rearrange("p (a n) -> p a n", a=QHP)
                v.wait_ge(score_done, QUARTERS * ph + i + 1)
                for m in range(QHP):
                    last = v.max(stop[:, m, 0:8], S[:, m, :])
                link(last)
                for m in range(QHP):
                    v.match_replace(S2[:, m, :], stop[:, m, 0:8], S[:, m, :], NEG)
                    last = v.max_index(itop[:, m, 0:8], stop[:, m, 0:8], S[:, m, :])
                link(last)

            def sum_pairs(ph, c, i):
                for m in range(QHP):
                    last = v.max(stop[:, m, 8:16], S2[:, m, :])
                link(last)
                for m in range(QHP):
                    last = v.max_index(itop[:, m, 8:16], stop[:, m, 8:16], S2[:, m, :])
                link(last)
                halves = stop.rearrange("p (h two) k -> p h two k", two=2)
                v.tensor_copy(itopf, itop)
                shape = [P, QH, TOPK, TOPK]
                link(v.tensor_tensor(cand.rearrange("p h (i j) -> p h i j", j=TOPK),
                                     spread(halves[:, :, 0, :], 3, shape),
                                     spread(halves[:, :, 1, :], 2, shape), ALU.add))

            def best_of_sums(ph, c, i):
                cand2 = S2.rearrange("p (h two) n -> p h (two n)", two=2)
                for h in range(QH):
                    last = v.max(best[:, h, 0:8], cand[:, h, :])
                link(last)
                for h in range(QH):
                    v.match_replace(cand2[:, h, :], best[:, h, 0:8], cand[:, h, :], NEG)
                    last = v.max_index(pos[:, h, 0:8], best[:, h, 0:8], cand[:, h, :])
                link(last)
                for h in range(QH):
                    last = v.max(best[:, h, 8:16], cand2[:, h, :])
                link(last)
                g3 = gate[:, c, QSTEPS * i:QSTEPS * (i + 1)].rearrange("p (h k) -> p h k", h=QH)
                v.tensor_tensor(g3, best, best[:, :, 0:1].to_broadcast([P, QH, TOPK]),
                                ALU.subtract).then_inc(best_ready, 1)
                for h in range(QH):
                    last = v.max_index(pos[:, h, 8:16], best[:, h, 8:16], cand2[:, h, :])
                link(last)

            def find_experts(ph, c, i):
                g3 = gate[:, c, QSTEPS * i:QSTEPS * (i + 1)].rearrange("p (h k) -> p h k", h=QH)
                ihalves = itopf.rearrange("p (h two) k -> p h two k", two=2)
                v.tensor_scalar(posi, pos, 4, None, ALU.logical_shift_right)
                link(v.tensor_scalar(posj, pos, TOPK - 1, None, ALU.bitwise_and))
                v.tensor_copy(posif, posi)
                link(v.tensor_copy(posjf, posj))
                flat = keyf.rearrange("p h k -> p (h k)")
                steps_i = slice(QSTEPS * i, QSTEPS * (i + 1))
                for src, half in ((posjf, 1), (posif, 0)):
                    shape = [P, QSTEPS, TOPK]
                    link(v.tensor_tensor(EQ[ph], spread(src.rearrange("p h k -> p (h k)"), 2, shape),
                                         spread(iota, 1, shape), ALU.is_equal))
                    eq4 = EQ[ph].rearrange("p (h k) i -> p h k i", h=QH)
                    link(v.tensor_tensor(eq4, eq4, spread(ihalves[:, :, half, :], 2,
                                                          [P, QH, TOPK, TOPK]), ALU.mult))
                    link(v.tensor_reduce(flat, EQ[ph], AX.X, ALU.add))
                    if half:
                        link(v.tensor_copy(row_b[:, c, steps_i], flat))
                v.tensor_scalar(row_a[:, c, steps_i], flat, float(NKEYS), None, ALU.mult)
                v.wait_ge(gate_exp, QUARTERS * ph + i + 1)
                link(v.tensor_reduce(gsum, g3, AX.X, ALU.add))
                link(v.reciprocal(grec, gsum))
                v.tensor_tensor(g3, g3, spread(grec, 2, [P, QH, TOPK]), ALU.mult).then_inc(idx_ready, 1)
                v.wait_ge(idx_ready, QUARTERS * ph + i + 1)

            def other_quarters(ph, apart):
                for i in range(1, QUARTERS):
                    for part in range(TOPK_PARTS):
                        g.at(ph, apart * (TOPK_PARTS * (i - 1) + part) + 1)
                        top_k_part(ph, i, part)

            def rope(c, half, j):
                n = 9 * (2 * c + half) + j
                m = 2 * (n // 3) + n % 3
                v.wait_ge(w_used, item(1, c, QKV + 9 * half + j) + 1)
                shape = [P, NH, DH]
                acc, ra, rb, rr = [t.rearrange("p (h e) -> p h e", h=NH)
                                   for t in (ps[:, 2 + j % 2, :], RA, RB, RR[m % 2])]
                cos = con[:, C_COS + DH * c:C_COS + DH * (c + 1)]
                sin = con[:, C_SIN + DH * c:C_SIN + DH * (c + 1)]
                v.tensor_tensor(ra, acc, spread(cos, 1, shape), ALU.mult)
                v.tensor_tensor(rb, acc, spread(sin, 1, shape), ALU.mult).then_inc(acc_evac, 1)
                v.wait_ge(acc_evac, n + 1)
                if m >= 2:
                    v.wait_ge(qk_turned, m - 1)
                lo, hi = slice(0, DH // 2), slice(DH // 2, DH)
                v.tensor_tensor(rr[:, :, lo], ra[:, :, lo], rb[:, :, hi], ALU.subtract)
                v.tensor_tensor(rr[:, :, hi], ra[:, :, hi], rb[:, :, lo], ALU.add).then_inc(roped, 1)

            def attn_mask(c, half, h):
                u, n = HEADS * c + NH * half + h, NG * P * (c + 1)
                v.wait_ge(s_done, u + 1)
                if u >= 2:
                    v.wait_ge(p_turned, u - 1)
                at = (1 - c) * 512 * (u % 2)
                v.tensor_tensor_reduce(SS[u % 2][:, 0:n], banks(2, 4)[:, at:at + n], mask[:, 0:n],
                                       1.0, NEG, ALU.add, ALU.max, mx[:, u:u + 1]).then_inc(s_masked, 1)
                v.wait_ge(s_masked, u + 1)
                v.tensor_scalar(nmx[:, u:u + 1], mx[:, u:u + 1], -(DH ** -0.5), None,
                                ALU.mult).then_inc(nmx_ready, 1)

            def attn_scale(c, half):
                u = HEADS * c + NH * half
                v.wait_ge(pv_done, u + NH)
                v.wait_ge(p_ready, u + NH)
                link(v.reciprocal(rden[:, u:u + NH], den[:, u:u + NH]))
                v.tensor_tensor(O[:, half * BLOCK:(half + 1) * BLOCK].rearrange("p (h e) -> p h e", h=NH),
                                ps[:, 7, :].rearrange("p (h e) -> p h e", h=NH),
                                spread(rden[:, u:u + NH], 2, [P, NH, DH]), ALU.mult).then_inc(o_scaled, 1)

            def layer1(gphase, c):
                norm(gphase, 0, c, norm_event(1, c, 0), normed, 0)
                for half in range(2):
                    base = QKV_AT + HALF_AT[c] * half
                    for n in range(1 if half == 0 else base + 1, base + 10):
                        g.at(gphase, n)
                        if half == 0 and n <= (QUARTERS - 1) * TOPK_PARTS:
                            i, part = divmod(n - 1, TOPK_PARTS)
                            top_k_part(gphase, i + 1, part)
                        j = n - base - 1
                        if j >= 0 and j % 3 < 2:
                            rope(c, half, j)
                    base = HEADS_AT[c] + HALF_AT[c] * half
                    if half == 0:
                        v.wait_ge(mask_in, 16 * (c + 1))
                    for i in range(1, NH + 1):
                        g.at(gphase, base + i // HEAD_TICKS[c])
                        attn_mask(c, half, i - 1)
                    g.at(gphase, base + (NH + 2) // HEAD_TICKS[c] + 1)
                    attn_scale(c, half)
                g.at(gphase, WO_AT[c] + 3)
                v.wait_ge(w_used, item(1, c, WO + 2))
                v.tensor_tensor(X[:, c, :], X[:, c, :], banks(4, 6), ALU.add).then_inc(wo_done, 1)
                v.wait_ge(wo_done, c + 1)
                norm(gphase, WO_AT[c] + 3, c, norm_event(1, c, 1), normed, 0)
                top_k(gphase, WO_AT[c] + 9, 2 + c, 0)

            s5_lambda()
            v.wait_ge(x_in[0], 16)
            norm(None, 0, 0, 0, normed, 0)
            layer0(None, 0)
            v.wait_ge(x_in[1], 16)
            norm(None, 0, 1, norm_event(0, 1, 0), normed, 0)
            other_quarters(0, 1)
            layer0(0, 1)
            peer_end(0)
            v.wait_ge(peer_done, 1)
            layer1(1, 0)
            peer_end(1)
            v.wait_ge(peer_done, 2)
            layer1(2, 1)
            peer_end(2)
            v.wait_ge(peer_done, 3)
            other_quarters(3, 3)
            norm(3, 3 * 3 * TOPK_PARTS + 4, 0, 8, out_ready, 0)
            peer_end(3)
            v.wait_ge(peer_done, 4)
            norm(None, 0, 1, 9, out_ready, 0)


def _constants():
    con = np.zeros((P, C_ALL), np.float32)
    con[:, C_ID:C_ID + P] = np.eye(P)
    con[:, C_RAMP:C_RAMP + P] = np.arange(1, P + 1)
    con[:, C_IOTA:C_IOTA + TOPK] = np.arange(TOPK)
    inv = np.float32(10000.0) ** (-np.arange(DH // 2, dtype=np.float32) / np.float32(DH // 2))
    ang = np.arange(SEQ, dtype=np.float32)[:, None] * inv.astype(np.float32)[None, :]
    for c in range(NC):
        a = np.tile(ang[c * P:(c + 1) * P], (1, 2))
        con[:, C_COS + DH * c:C_COS + DH * (c + 1)] = np.cos(a)
        con[:, C_SIN + DH * c:C_SIN + DH * (c + 1)] = np.sin(a)
    masks = np.zeros((P, M_ALL), np.float32)
    for c in range(NC):
        n = P * (c + 1)
        for g, (window, dilation) in enumerate(DILATED):
            dist = (c * P + np.arange(P))[:, None] - np.arange(n)[None, :]
            seen = (dist >= 0) & (dist <= window) & (dist % dilation == 0)
            masks[:, M_AT[c] + g * n:M_AT[c] + (g + 1) * n] = np.where(seen, 0.0, MASKED)
    return con, masks


def _layout(i):
    con, masks = _constants()
    def by_state(t):
        return t.reshape(PAIRS, 2, STATE).transpose(1, 2, 0).reshape(P, PAIRS)
    step = np.repeat(i["s5_log_step"][0], STATE).reshape(GROUPS, STATE)
    lam = np.stack([by_state(i["s5_lam_re"][0]), by_state(i["s5_lam_im"][0]), by_state(step)], 1)
    b = np.stack([i["s5_b_re"][0], i["s5_b_im"][0]])
    b = b.reshape(2, KT, 8, STATE, GH).transpose(0, 2, 4, 1, 3)
    c = np.stack([i["s5_c_re"][0], i["s5_c_im"][0]])
    c = c.reshape(2, PAIRS, 2, GH, STATE).transpose(2, 4, 0, 1, 3).reshape(P, 2, PAIRS, GH)
    return {
        "x": i["x"].reshape(SEQ, D),
        "gains": np.stack([i["norm_mix"][0], i["norm_ffn"][0], i["norm_mix"][1], i["norm_ffn"][1],
                           i["norm_final"]]),
        "lam": lam, "b_in": b, "c_out": c,
        "d_skip": i["s5_d"][0].reshape(KT, P).T,
        "w_glu": i["s5_w_glu"][0], "w_qkv": i["attn_w_qkv"][0], "w_o": i["attn_w_o"][0],
        "w_q": i["peer_w_q"],
        "keys": i["peer_sub_keys"].reshape(2, HP, NKEYS, P).transpose(0, 3, 1, 2),
        "experts0": np.concatenate([i["peer_u"][0], i["peer_v"][0]], axis=1),
        "experts1": np.concatenate([i["peer_u"][1], i["peer_v"][1]], axis=1),
        "consts": con, "masks": masks,
    }


def kernel(**inputs):
    import concourse.bacc as bacc
    from concourse.bass_utils import run_bass_kernel_spmd

    arrays = {k: np.ascontiguousarray(a) for k, a in
              _layout({k: np.asarray(v) for k, v in inputs.items()}).items()}
    nc = bacc.Bacc("TRN2", target_bir_lowering=False, num_devices=1)
    ap = {k: nc.dram_tensor(k, a.shape, mybir.dt.from_np(a.dtype), kind="ExternalInput").ap()
          for k, a in arrays.items()}
    out = nc.dram_tensor("out", (SEQ, D), F32, kind="ExternalOutput").ap()
    ap["experts"] = [ap.pop("experts0"), ap.pop("experts1")]
    build(nc, out=out, **ap)
    r = run_bass_kernel_spmd(nc, [arrays], core_ids=[0])
    return r.results[0]["out"].reshape(1, SEQ, D)
```
